# Optimizing a Trainium2 kernel written in Bass

```python
import math
import jax, jax.numpy as jnp
from jax import lax
import numpy as np

D_MODEL = 1024
BATCH = 1
SEQ = 128
DEPTH = 2
DEC_BATCH = 1
DEC_SEQ = 512
PAST_LEN = 128

GRID_W = 64
HEAD_DIM = 64
NA_HEADS = 8
NA_WIDTH = NA_HEADS * HEAD_DIM
FNET_GROUPS = 4
FNET_GROUP_DIM = 128
FNET_WIDTH = FNET_GROUPS * FNET_GROUP_DIM
WIN_ROWS = 8
WIN_COLS = 16
D_FF = 2816
N_SUB = 3
N_MOD = 3 * N_SUB
IN_WIDTH = 3 * NA_WIDTH + FNET_WIDTH + 2 * D_MODEL
Q_BLOCK = 128
ATTN_SCALE = HEAD_DIM ** -0.5
ALPHA = (2 * DEPTH) ** 0.25
BETA = (8 * DEPTH) ** -0.25
LN_EPS = 1e-5
NEG_INF = -1e30

kernel_name = 'hybrid_fnet_natten_macaron_deepnorm_step'

def _layer_norm(x, g, b):
    xf = x.astype(jnp.float32)
    mu = jnp.mean(xf, axis=-1, keepdims=True)
    var = jnp.mean(jnp.square(xf - mu), axis=-1, keepdims=True)
    y = (xf - mu) * lax.rsqrt(var + LN_EPS)
    return (y * g.astype(jnp.float32) + b.astype(jnp.float32)).astype(x.dtype)

def _mods(cvec, w_ada, b_ada):
    m = jax.nn.silu(cvec) @ w_ada + b_ada
    return m.reshape(cvec.shape[0], 1, N_MOD, D_MODEL)

def _modulate(x, mods, i):
    return x * (1.0 + mods[:, :, 3 * i + 1]) + mods[:, :, 3 * i]

def _post_norm(x, y, mods, i, res_w, ln_g, ln_b):
    return _layer_norm(ALPHA * x + res_w * mods[:, :, 3 * i + 2] * y, ln_g[i], ln_b[i])

def _swiglu(u, w_up, w_down):
    a, g = jnp.split(u @ w_up, 2, axis=-1)
    return (jax.nn.silu(g) * a) @ w_down

def _ffn_sublayer(x, mods, i, w_up, w_down, ln_g, ln_b):
    y = _swiglu(_modulate(x, mods, i), w_up, w_down)
    return _post_norm(x, y, mods, i, 0.5, ln_g, ln_b)

def _heads(t):
    b_, l_ = t.shape[:2]
    return t.reshape(b_, l_, NA_HEADS, HEAD_DIM).transpose(0, 2, 1, 3)

def _merge_heads(o):
    b_, _, l_, _ = o.shape
    return o.transpose(0, 2, 1, 3).reshape(b_, l_, NA_WIDTH)

def _project_in(u, w_in):
    z = u @ w_in
    cuts = [NA_WIDTH, 2 * NA_WIDTH, 3 * NA_WIDTH, 3 * NA_WIDTH + FNET_WIDTH,
            3 * NA_WIDTH + FNET_WIDTH + D_MODEL]
    q, k, v, f, g_a, g_b = jnp.split(z, cuts, axis=-1)
    return _heads(q) * ATTN_SCALE, _heads(k), _heads(v), f, g_a, g_b

def _fourier_mix(f):
    b_, l_ = f.shape[:2]
    fg = f.reshape(b_, l_, FNET_GROUPS, FNET_GROUP_DIM).transpose(0, 2, 1, 3).astype(jnp.float32)
    y = jnp.fft.fft2(fg, norm='ortho').real
    return y.transpose(0, 2, 1, 3).reshape(b_, l_, FNET_WIDTH).astype(f.dtype)

def _merge_branches(f, o_na, g_a, g_b, w_fourier, w_na_out, w_out):
    branch_a = _fourier_mix(f) @ w_fourier
    branch_b = _merge_heads(o_na) @ w_na_out
    return (jax.nn.sigmoid(g_a) * branch_a + jax.nn.sigmoid(g_b) * branch_b) @ w_out

def _context_attention(q, k, v):
    b_, h_, lc, hd = q.shape
    nblk = lc // Q_BLOCK
    qb = q.reshape(b_, h_, nblk, Q_BLOCK, hd).transpose(2, 0, 1, 3, 4)

    def one_block(qi):
        s = jnp.einsum('bhqd,bhkd->bhqk', qi, k).astype(jnp.float32)
        p = jax.nn.softmax(s, axis=-1).astype(v.dtype)
        return jnp.einsum('bhqk,bhkd->bhqd', p, v)

    o = lax.map(one_block, qb)
    return o.transpose(1, 2, 0, 3, 4).reshape(b_, h_, lc, hd)

def _neighbourhood_attention(q, k, v, k_ctx, v_ctx, rpb):
    b_, h_, l_, hd = q.shape
    rows = l_ // GRID_W
    kr = min(WIN_ROWS, rows)
    qg = q.reshape(b_, h_, rows, GRID_W, hd)
    kg = k.reshape(b_, h_, rows, GRID_W, hd)
    vg = v.reshape(b_, h_, rows, GRID_W, hd)
    r_idx = jnp.arange(rows)
    r0 = jnp.clip(r_idx - kr // 2, 0, rows - kr)
    key_rows = r0[:, None] + jnp.arange(kr)[None, :]
    k_band = jnp.take(kg, key_rows, axis=2)
    v_band = jnp.take(vg, key_rows, axis=2)
    c_idx = jnp.arange(GRID_W)
    c0 = jnp.clip(c_idx - WIN_COLS // 2, 0, GRID_W - WIN_COLS)
    col_ok = (c_idx[None, :] >= c0[:, None]) & (c_idx[None, :] < c0[:, None] + WIN_COLS)
    dr = key_rows - r_idx[:, None] + (WIN_ROWS - 1)
    dc = jnp.clip(c_idx[None, :] - c_idx[:, None] + (WIN_COLS - 1), 0, 2 * WIN_COLS - 2)
    bias = rpb[:, dr[:, None, :, None], dc[None, :, None, :]].astype(jnp.float32)
    s_win = jnp.einsum('bhrqd,bhrkcd->bhrqkc', qg, k_band).astype(jnp.float32) + bias[None]
    s_win = jnp.where(col_ok[:, None, :], s_win, NEG_INF)
    s_ctx = jnp.einsum('bhrqd,bhjd->bhrqj', qg, k_ctx).astype(jnp.float32)
    n_win = kr * GRID_W
    s = jnp.concatenate([s_win.reshape(b_, h_, rows, GRID_W, n_win), s_ctx], axis=-1)
    p = jax.nn.softmax(s, axis=-1).astype(v.dtype)
    p_win = p[..., :n_win].reshape(b_, h_, rows, GRID_W, kr, GRID_W)
    p_ctx = p[..., n_win:]
    o = (jnp.einsum('bhrqkc,bhrkcd->bhrqd', p_win, v_band)
         + jnp.einsum('bhrqj,bhjd->bhrqd', p_ctx, v_ctx))
    return o.reshape(b_, h_, l_, hd)

def setup_inputs(seed: int = 0) -> dict:
    key = jax.random.key(seed)
    ks = jax.random.split(key, 20)
    nrm = lambda k_, shape, s: jax.random.normal(k_, shape, jnp.float32) * s
    return {
        'x_prompt': nrm(ks[0], (BATCH, SEQ, D_MODEL), 1.0),
        'x_sample': nrm(ks[1], (DEC_BATCH, DEC_SEQ, D_MODEL), 1.0),
        'cache_k': nrm(ks[2], (DEC_BATCH, DEPTH, NA_HEADS, PAST_LEN, HEAD_DIM), 1.0),
        'cache_v': nrm(ks[3], (DEC_BATCH, DEPTH, NA_HEADS, PAST_LEN, HEAD_DIM), 1.0),
        'c': nrm(ks[4], (DEC_BATCH, D_MODEL), 1.0),
        'c_ctx': nrm(ks[5], (D_MODEL,), 1.0),
        'w_ada': nrm(ks[6], (DEPTH, D_MODEL, N_MOD * D_MODEL), 0.5 * D_MODEL ** -0.5),
        'b_ada': nrm(ks[7], (DEPTH, N_MOD * D_MODEL), 0.01),
        'ln_g': 1.0 + nrm(ks[8], (DEPTH, N_SUB, D_MODEL), 0.01),
        'ln_b': nrm(ks[9], (DEPTH, N_SUB, D_MODEL), 0.01),
        'w_ff1_up': nrm(ks[10], (DEPTH, D_MODEL, 2 * D_FF), D_MODEL ** -0.5),
        'w_ff1_down': nrm(ks[11], (DEPTH, D_FF, D_MODEL), BETA * D_FF ** -0.5),
        'w_in': nrm(ks[12], (DEPTH, D_MODEL, IN_WIDTH), D_MODEL ** -0.5),
        'rpb': nrm(ks[13], (DEPTH, NA_HEADS, 2 * WIN_ROWS - 1, 2 * WIN_COLS - 1), 0.02),
        'w_fourier': nrm(ks[14], (DEPTH, FNET_WIDTH, D_MODEL), BETA * FNET_WIDTH ** -0.5),
        'w_na_out': nrm(ks[15], (DEPTH, NA_WIDTH, D_MODEL), BETA * NA_WIDTH ** -0.5),
        'w_out': nrm(ks[16], (DEPTH, D_MODEL, D_MODEL), BETA * D_MODEL ** -0.5),
        'w_ff2_up': nrm(ks[17], (DEPTH, D_MODEL, 2 * D_FF), D_MODEL ** -0.5),
        'w_ff2_down': nrm(ks[18], (DEPTH, D_FF, D_MODEL), BETA * D_FF ** -0.5),
    }

def reference(x_prompt, x_sample, cache_k, cache_v, c, c_ctx, w_ada, b_ada, ln_g, ln_b,
              w_ff1_up, w_ff1_down, w_in, rpb, w_fourier, w_na_out, w_out, w_ff2_up, w_ff2_down):
    y_p = x_prompt
    y_s = x_sample
    k_list, v_list = [], []
    for l in range(DEPTH):
        m_ctx = _mods(c_ctx[None, :], w_ada[l], b_ada[l])
        m_lat = _mods(c, w_ada[l], b_ada[l])

        y_p = _ffn_sublayer(y_p, m_ctx, 0, w_ff1_up[l], w_ff1_down[l], ln_g[l], ln_b[l])
        q, k, v, f, g_a, g_b = _project_in(_modulate(y_p, m_ctx, 1), w_in[l])
        o = _context_attention(q, k, v)
        mix = _merge_branches(f, o, g_a, g_b, w_fourier[l], w_na_out[l], w_out[l])
        y_p = _post_norm(y_p, mix, m_ctx, 1, 1.0, ln_g[l], ln_b[l])
        y_p = _ffn_sublayer(y_p, m_ctx, 2, w_ff2_up[l], w_ff2_down[l], ln_g[l], ln_b[l])
        k_list.append(k)
        v_list.append(v)

        y_s = _ffn_sublayer(y_s, m_lat, 0, w_ff1_up[l], w_ff1_down[l], ln_g[l], ln_b[l])
        q, k, v, f, g_a, g_b = _project_in(_modulate(y_s, m_lat, 1), w_in[l])
        o = _neighbourhood_attention(q, k, v, cache_k[:, l], cache_v[:, l], rpb[l])
        mix = _merge_branches(f, o, g_a, g_b, w_fourier[l], w_na_out[l], w_out[l])
        y_s = _post_norm(y_s, mix, m_lat, 1, 1.0, ln_g[l], ln_b[l])
        y_s = _ffn_sublayer(y_s, m_lat, 2, w_ff2_up[l], w_ff2_down[l], ln_g[l], ln_b[l])

    new_k = jnp.stack(k_list, axis=1)
    new_v = jnp.stack(v_list, axis=1)
    return (y_p, y_s, new_k, new_v)


_drawn_inputs = setup_inputs


def setup_inputs(seed=0):
    import zlib

    import numpy as np

    out = dict(_drawn_inputs(seed))
    spreads = {}
    factors = {'cache_k': 8.0, 'cache_v': 8.0, 'b_ada': 4.264, 'rpb': 8.0, 'w_na_out': 3.68}
    for name, (base, spread) in spreads.items():
        noise = np.random.default_rng([zlib.crc32(name.encode()), seed]).standard_normal(out[name].shape)
        drawn = base * np.exp(spread * noise) if base else spread * noise
        out[name] = __import__('jax').numpy.asarray(drawn.astype(out[name].dtype))
    for name, factor in factors.items():
        out[name] = (out[name] * factor).astype(out[name].dtype)
    return out
```

```python
import numpy as np
from contextlib import ExitStack

import concourse.bass as bass
import concourse.mybir as mybir

F32 = mybir.dt.float32
F32R = mybir.dt.float32r
BF16 = mybir.dt.bfloat16
ALU = mybir.AluOpType
ACT = mybir.ActivationFunctionType
AX_X = mybir.AxisListType.X

P = 128
D = 1024
KD = D // P
DEPTH = 2
LAT, CTX = 512, 128
T = LAT + CTX
HT = T // 2
FF = 2816
HEADS, HD = 8, 64
NA = HEADS * HD
GRID_W, ROWS = 64, LAT // 64
WIN = 16
ATTN_SCALE = HD ** -0.5
ALPHA = (2 * DEPTH) ** 0.25
LN_EPS = 1e-5
NEG = -1e30

GROUPS = (8, 8, 6)
QTILE = 16
QB = GRID_W // QTILE
WCOLS = 32
KEY0 = (0, 8, 24, 32)
VTILES = ((0, 1), (4, 5), (5, 6), (2, 3))
BIAS_KIND = (0, 1, 1, 2)
BIAS_OFF = (16, 8, 0)
TW = 48
RW = 64
SEGS = (((0, HT, 0),), ((HT, LAT, 0), (LAT, T, 1)))

ADA_SUB = 3 * KD
TILES = 92
USES = 264

FFN_USES, MIX_GATES = 44, 8


class Count:

    def __init__(self, sem, per_layer, first=0):
        self.sem, self.per_layer, self.first = sem, per_layer, first
        self.base, self.n = first, 0

    def at(self, back=0):
        return self.base + (self.n - back)

    def next(self, k=1):
        self.n += k
        return self.at()


def over(eng, trips, steps, body, met):
    met()
    kept = [(c, c.base, c.n) for c, _ in steps]
    with eng.Fori(0, trips) as i:
        for c, s in steps:
            c.base, c.n = eng.snap(c.at() + i * s), 0
        body(i)
        for c, s in steps:
            assert c.n == s, (c.sem, c.n, s)
    for (c, base, n), (_, s) in zip(kept, steps):
        c.base, c.n = base, n + trips * s


def over_layers(eng, counts, body):
    with eng.Fori(0, DEPTH) as layer:
        for c in counts:
            c.base, c.n = eng.snap(layer * c.per_layer + c.first), 0
        body(layer)
        for c in counts:
            assert c.n == c.per_layer, (c.sem, c.n, c.per_layer)
    for c in counts:
        c.base, c.n = c.first + DEPTH * c.per_layer, 0


def build(nc, a):
    ctx = ExitStack()
    with ctx:
        def sb(name, shape, dt=F32):
            return ctx.enter_context(nc.sbuf_tensor(name, shape, dt))

        def sem(name):
            return ctx.enter_context(nc.semaphore(name))

        X = sb("X", [P, KD, T])
        Uh = sb("Uh", [P, KD, T], F32R)
        Ul = sb("Ul", [P, KD, T], F32R)
        w_raw = sb("w_raw", [P, 2, 16, P])
        w_hi = sb("w_hi", [P, 2, 16, P], F32R)
        w_lo = sb("w_lo", [P, 2, 16, P], F32R)
        ada_w = sb("ada_w", [P, 2, D])
        junk = sb("junk", [P, D], BF16)
        csilu = sb("csilu", [P, 2, D])
        cst_h = sb("cst_h", [P, 4, P], F32R)
        cst_l = sb("cst_l", [P, 4, P], F32R)
        ident = sb("ident", [P, P])
        ones = sb("ones", [P, P])
        lng = sb("lng", [P, DEPTH * 3 * KD])
        lnb = sb("lnb", [P, DEPTH * 3 * KD])
        bada = sb("bada", [P, (1 + DEPTH * 3) * ADA_SUB])
        mods = [sb(f"mods{s}", [P, 2, ADA_SUB]) for s in range(3)]
        acc4 = sb("acc4", [P, 2, 2])
        epsc = sb("epsc", [P, 1])
        zone_bytes = 75776
        z0 = -(-nc.sbuf_base // 32) * 32
        sb("zone", [P, zone_bytes // 4 + 8])

        def at(name, off, shape, dt=F32):
            size = 4 * int(np.prod(shape[1:]))
            assert off + size <= zone_bytes, (name, off + size)
            return nc.alloc_sbuf_tensor_at(name, shape, dt, offset=z0 + off)

        Hh = at("Hh", 0, [P, 8, T], F32R)
        Hl = at("Hl", 20480, [P, 8, T], F32R)
        sg = at("sg", 40960, [P, 2, HT])
        hf = at("hf", 43520, [P, 2, HT])
        sq = at("sq", 0, [P, KD, T])
        std = at("std", 46080, [P, 2, HT])
        u32 = at("u32", 48640, [P, 4, HT])
        craw = at("craw", 0, [P, 2, D])
        cst = at("cst", 8192, [P, 4, P])
        o32 = at("o32", 0, [P, 4, T])
        y32 = at("y32", 10240, [P, 4, T])
        qT = at("qT", 20480, [P, 2, T])
        kT = at("kT", 25600, [P, 2, T])
        ckT = at("ckT", 30720, [P, 4, P])
        V = at("V", 32768, [P, 9, 256])
        G = at("G", 41984, [P, 4, ROWS, TW])
        mask = at("mask", 48128, [P, 3, 256])
        bm = at("bm", 51200, [P, 3, 256])
        pr = at("pr", 54272, [P, 3, 384])
        PT = at("PT", 58880, [P, 3, 384])
        stat = at("stat", 63488, [P, 4, 4])
        Fh = at("Fh", 20480, [P, 5, NA], F32R)
        Fl = at("Fl", 30720, [P, 5, NA], F32R)
        PCh = at("PCh", 40960, [P, 4, LAT], F32R)
        PCl = at("PCl", 49152, [P, 4, LAT], F32R)
        PSh = at("PSh", 57344, [P, 4, LAT], F32R)
        PSl = at("PSl", 65536, [P, 4, LAT], F32R)
        CXh = at("CXh", 57344, [P, 4, 256], F32R)
        CXl = at("CXl", 61440, [P, 4, 256], F32R)
        Oh = at("Oh", 20480, [P, 4, T], F32R)
        Ol = at("Ol", 30720, [P, 4, T], F32R)
        Yh = at("Yh", 40960, [P, 4, T], F32R)
        Yl = at("Yl", 51200, [P, 4, T], F32R)
        sig = at("sig", 61440, [P, 4, 2, HT])
        ta = at("ta", 71680, [P, 2, HT])
        M32 = at("M32", 0, [P, KD, T])
        Mh = at("Mh", 20480, [P, KD, T], F32R)
        Ml = at("Ml", 40960, [P, KD, T], F32R)

        psum = ctx.enter_context(nc.psum_tensor("psum", [P, 8, 512], F32))

        def bank(u, b, lo, hi, p0=0, p1=P):
            return psum[p0:p1, 2 * (u % 4) + b, lo:hi]

        s_x = sem("x_loaded")
        s_cst = sem("const_loaded")
        s_gath = sem("bias_gathered")
        s_wload = [sem(f"w_loaded{s}") for s in range(2)]
        s_whi = sem("w_hi_done")
        s_wsplit = sem("w_split")
        s_wstart = sem("w_tile_started")
        s_aload = [sem(f"ada_loaded{s}") for s in range(2)]
        s_adone = sem("ada_chunk_done")
        s_csilu = sem("csilu_done")
        s_init = sem("constants_ready")
        s_full = sem("psum_full")
        s_free = sem("psum_free")
        s_func = sem("function_done")
        s_h = sem("hidden_ready")
        s_dve = sem("vector_step")
        s_mods = sem("mods_ready")
        s_u32 = sem("modulated")
        s_u = sem("u_ready")
        s_mean = sem("mean_ready")
        s_xc = sem("centred")
        s_sq = sem("squared")
        s_xn = sem("normed")
        s_y = sem("post_norm_done")
        s_att = sem("attention_inputs")
        s_max = sem("max_ready")
        s_cc = sem("cached_scores_copied")
        s_exp = sem("exp_done")
        s_o = sem("head_output_ready")
        s_p = sem("probs_ready")
        s_pt = sem("probs_transposed")
        s_ptc = sem("probs_copied")
        s_mix = sem("branch_inputs_split")
        s_mrg = sem("merged_split")
        s_kv = sem("kv_stored")
        s_out = sem("y_stored")

        def pool_met(s):
            nc.gpsimd.sem_inc(s_stands["pool"], 1)

        def pe_met():
            nc.tensor.sem_inc(s_stands["pe"], 1)

        def act_met():
            nc.scalar.sem_inc(s_stands["act"], 1)

        def dve_met():
            nc.vector.sem_inc(s_stands["dve"], 1)

        s_stands = {e: sem("wait_taken_" + e) for e in ("pool", "pe", "act", "dve")}
        block = ctx.enter_context(nc.Block())

        def make(which):
            per = dict(PER_LAYER)
            sems = dict(
                tile=s_wstart, use=s_free, full=s_full, func=s_func, h=s_h, mods=s_mods, u32=s_u32,
                u=s_u, mean=s_mean, xc=s_xc, sq=s_sq, xn=s_xn, y=s_y, att=s_att, max=s_max,
                cc=s_cc, exp=s_exp, p=s_p, pt=s_pt, ptc=s_ptc, o=s_o, mix=s_mix, mrg=s_mrg,
                kv=s_kv, ada=s_adone, dve=s_dve)
            first = dict(use=4, tile=1, ada=ADA_SUB, mods=1, u=2 * KD, u32=2 * KD, dve=FIRST_DVE)
            return {k: Count(sems[k], per[k], first.get(k, 0)) for k in which}

        @block.sync
        def _(sp):
            for k in range(KD):
                sp.dma_start(X[:, k, :], a["xT"][k]).then_inc(s_x, 16)
            sp.dma_start(cst[:, :, :], a["dft_small"]).then_inc(s_cst, 16)
            sp.dma_start(ident[:, :], a["eye"]).then_inc(s_cst, 16)
            sp.dma_start(lng[:, :], a["lng"]).then_inc(s_cst, 16)
            sp.dma_start(lnb[:, :], a["lnb"]).then_inc(s_cst, 16)
            for s in range(2):
                sp.dma_start(w_raw[:, s, :, :], a["wstream"][s]).then_inc(s_wload[s], 16)
            for c in range(QTILE):
                for r in range(ROWS):
                    src = a["rpb"][:, ROWS - 1 - r:2 * ROWS - 1 - r, QTILE - 1 - c:QTILE - 1 - c + TW]
                    sp.dma_start(a["gath"][:, c * ROWS + r, :, :], src).then_inc(s_gath, 16)
            with sp.Fori(1, DEPTH * TILES // 2) as j:
                for s in range(2):
                    sp.wait_ge(s_wsplit, j * 2 + (s - 1))
                    sp.dma_start(w_raw[:, s, :, :], a["wstream"][j * 2 + s]).then_inc(s_wload[s], 16)
            sp.wait_ge(s_y, DEPTH * PER_LAYER["y"])
            for k in range(KD):
                sp.dma_start(a["yT"][k], X[:, k, :]).then_inc(s_out, 16)
            sp.wait_ge(s_out, 16 * KD)

        @block.gpsimd
        def _(pool):
            with pool.Fori(0, DEPTH * TILES // 2) as j:
                for s in range(2):
                    pool.wait_ge(s_wload[s], j * 16 + 16)
                    pool.wait_ge(s_wstart, j * 2 + (s + 1))
                    pool_met(s)
                    pool.tensor_scalar(w_hi[:, s, :, :], w_raw[:, s, :, :], 1.0, 0.0, ALU.mult,
                                       ALU.add).then_inc(s_whi, 1)
                    pool.wait_ge(s_whi, j * 2 + (s + 1))
                    pool.tensor_tensor(w_lo[:, s, :, :], w_raw[:, s, :, :],
                                       w_hi[:, s, :, :].bitcast(F32), ALU.subtract).then_inc(s_wsplit, 1)

        @block.tensor
        def _(pe):
            C = make("tile use full h u mean sq att p pt ptc o mix mrg".split())
            tile, use = C["tile"], C["use"]
            slot = [0]

            def products(out, left, right, first, last):
                (lh, ll), (rh, rl) = left, right
                pe.matmul(out, lh, rh, start=first, stop=False)
                pe.matmul(out, lh, rl, start=False, stop=False)
                return pe.matmul(out, ll, rh, start=False, stop=last)

            class Tiles:

                def __init__(self):
                    self.left = 0

                def block(self, n=1, as_moving=False):
                    if self.left == 0:
                        pe.wait_ge(s_wsplit, tile.at())
                        self.left, self.fresh = 16, True
                        self.s = slot[0]
                        slot[0] ^= 1
                    b = 16 - self.left
                    self.left -= n
                    view = [w[:, self.s, b:b + n, :] for w in (w_hi, w_lo)]
                    return view

                def started(self, mm):
                    if self.fresh:
                        mm.then_inc(s_wstart, 1)
                        tile.next()
                        self.fresh = False

            use_no = [0]

            def next_use():
                pe.wait_ge(s_free, use.at(3))
                use.next()
                use_no[0] += 1
                return use_no[0] - 1

            def all_evacuated():
                pe.wait_ge(s_free, use.at())

            def filled(mm):
                mm.then_inc(s_full, 1)
                C["full"].next()

            def stationary(tiles, outs, moving, nk):
                for k in range(nk):
                    wh, wl = tiles.block()
                    wh, wl = wh[:, 0, :], wl[:, 0, :]
                    for i, (out, mv) in enumerate(zip(outs, moving)):
                        rh, rl = mv(k)
                        m1 = pe.matmul(out, wh, rh, start=(k == 0), stop=False)
                        tiles.started(m1)
                        pe.matmul(out, wh, rl, start=False, stop=False)
                        mm = pe.matmul(out, wl, rh, start=False, stop=(k == nk - 1))
                return mm

            def half(th, tl, h):
                return lambda k: (th[:, k, h * HT:(h + 1) * HT], tl[:, k, h * HT:(h + 1) * HT])

            def norm():
                u = [next_use(), next_use()]
                pe.wait_ge(s_free, use.at(2))
                for h in range(2):
                    for k in range(KD):
                        mm = pe.matmul(bank(u[h], 0, 0, HT), ones[:, :], X[:, k, h * HT:(h + 1) * HT],
                                       start=(k == 0), stop=(k == KD - 1))
                    mm.then_inc(s_mean, 1)
                for h in range(2):
                    for k in range(KD):
                        pe.wait_ge(s_sq, C["sq"].next())
                        mm = pe.matmul(bank(u[h], 1, 0, HT), ones[:, :], sq[:, k, h * HT:(h + 1) * HT],
                                       start=(k == 0), stop=(k == KD - 1))
                    filled(mm)
                C["mean"].next(2)

            def down(nk, mh, ml, n0, n1, tiles):
                for n in range(n0, n1):
                    u = next_use()
                    mm = stationary(tiles, [bank(u, h, 0, HT) for h in range(2)],
                                    [half(mh, ml, h) for h in range(2)], nk)
                    filled(mm)

            def pairs(trips, tiles_per, uses_per, body, extra=()):
                assert tiles_per % 2 == 0 and uses_per % 4 == 0
                start = use_no[0]
                over(pe, trips, [(tile, tiles_per), (use, uses_per), (C["full"], uses_per)]
                     + list(extra), body, pe_met)
                use_no[0] = start + uses_per * trips

            def ffn():
                for size in GROUPS:
                    def up(i):
                        tiles = Tiles()
                        for m in range(2):
                            pair = tiles.block(16)
                            for h in range(2):
                                u = next_use()
                                for b in range(2):
                                    for k in range(KD):
                                        wh, wl = [w[:, b * KD + k, :] for w in pair]
                                        rh, rl = half(Uh, Ul, h)(k)
                                        out = bank(u, b, 0, HT)
                                        m1 = pe.matmul(out, wh, rh, start=(k == 0), stop=False)
                                        tiles.started(m1)
                                        pe.matmul(out, wh, rl, start=False, stop=False)
                                        mm = pe.matmul(out, wl, rh, start=False, stop=(k == KD - 1))
                                filled(mm)

                    pe.wait_ge(s_u, C["u"].at())
                    pairs(size // 2, 2, 4, up)
                    pe.wait_ge(s_h, C["h"].next(2 * size))
                    if size == 8:
                        pairs(2, 2, 4, lambda i: down(8, Hh, Hl, 0, 4, Tiles()))
                    else:
                        down(size, Hh, Hl, 0, KD, Tiles())
                norm()
                C["u"].next(2 * KD)

            def attention():
                units = [(h, j) for h in range(4) for j in range(QB)] + [(h, QB) for h in range(4)]
                u0 = use_no[0]
                n = len(units)
                for i in range(n + 3):
                    if i < n:
                        h, j = units[i]
                        u = next_use()
                        po, hp = HD * (h % 2), h // 2
                        if j < QB:
                            q = qT[po:po + HD, hp, j * P:(j + 1) * P]
                            pe.matmul(bank(u, 0, 0, 256), q,
                                      kT[po:po + HD, hp, KEY0[j] * ROWS:KEY0[j] * ROWS + 256],
                                      start=True, stop=True)
                            mm = pe.matmul(bank(u, 1, 384, 512), q,
                                           ckT[po:po + HD, 2 * att_half[0] + hp, :], start=True, stop=True)
                        else:
                            mm = pe.matmul(bank(u, 0, 0, P), qT[po:po + HD, hp, LAT:T],
                                           kT[po:po + HD, hp, LAT:T], start=True, stop=True)
                        filled(mm)
                    if 2 <= i < n + 2:
                        h, j = units[i - 2]
                        u = u0 + i - 2
                        pe.wait_ge(s_p, C["p"].next())
                        for t in range(3 if j < QB else 1):
                            mm = pe.transpose(bank(u, 1, t * P, (t + 1) * P), pr[:, (i - 2) % 3, t * P:(t + 1) * P],
                                              ident[:, :])
                        mm.then_inc(s_pt, 1)
                        C["pt"].next()
                    if 3 <= i:
                        h, j = units[i - 3]
                        u = u0 + i - 3
                        po = HD * (h % 2)
                        pe.wait_ge(s_ptc, C["ptc"].next())
                        vt = VTILES[j] + (8,) if j < QB else (7,)
                        for t, v in enumerate(vt):
                            mm = pe.matmul(bank(u, 0, 384, 512, po, po + HD), V[:, v, h * HD:(h + 1) * HD],
                                           PT[:, (i - 3) % 3, t * P:(t + 1) * P],
                                           start=(t == 0), stop=(t == len(vt) - 1))
                        mm.then_inc(s_o, 1)
                        C["o"].next()

            att_half = [0]

            def token_major():
                wh, wl = [w.rearrange("p (k c) n -> p k (c n)", k=KD) for w in vf_tiles.block(16)]
                for t in range(T // P):
                    u = next_use()
                    for k in range(KD):
                        uh, ul = Uh[:, k, t * P:(t + 1) * P], Ul[:, k, t * P:(t + 1) * P]
                        out = bank(u, 0, 0, 256)
                        m1 = pe.matmul(out, uh, wh[:, k, :], start=(k == 0), stop=False)
                        vf_tiles.started(m1)
                        pe.matmul(out, uh, wl[:, k, :], start=False, stop=False)
                        mm = pe.matmul(out, ul, wh[:, k, :], start=False, stop=(k == KD - 1))
                    filled(mm)

            vf_tiles = Tiles()

            def fourier():
                for part in range(2):
                    wh, wl = [w.rearrange("p (k c) n -> p k (c n)", k=4) for w in vf_tiles.block(16)]
                    if part == 0:
                        all_evacuated()
                    for g in range(4):
                        u = next_use()
                        for kt in range(4):
                            fh, fl = [f[:, kt, g * P:(g + 1) * P] for f in (Fh, Fl)]
                            out = bank(u, 0, 0, LAT)
                            m1 = pe.matmul(out, fh, wh[:, kt, :], start=(kt == 0), stop=False)
                            vf_tiles.started(m1)
                            pe.matmul(out, fh, wl[:, kt, :], start=False, stop=False)
                            mm = pe.matmul(out, fl, wh[:, kt, :], start=False, stop=(kt == 3))
                        filled(mm)
                for g in range(4):
                    if g == 0:
                        all_evacuated()
                    u = next_use()
                    out = bank(u, 0, 0, LAT)
                    products(out, (cst_h[:, 0, :], cst_l[:, 0, :]), (PCh[:, g, :], PCl[:, g, :]), True, False)
                    filled(products(out, (cst_h[:, 1, :], cst_l[:, 1, :]), (PSh[:, g, :], PSl[:, g, :]),
                                    False, True))
                u = next_use()
                ch, cl = [c[:, 2:4, :] for c in (cst_h, cst_l)]
                for g in range(4):
                    fh, fl = [f[:, 4, g * P:(g + 1) * P] for f in (Fh, Fl)]
                    mm = products(bank(u, g // 2, 256 * (g % 2), 256 * (g % 2) + 256), (fh, fl), (ch, cl), True, True)
                filled(mm)
                all_evacuated()
                u = next_use()
                out = bank(u, 0, 0, LAT).rearrange("p (g n) -> p g n", g=4)
                products(out, (cst_h[:, 0, :], cst_l[:, 0, :]), (CXh[:, :, 0:P], CXl[:, :, 0:P]), True, False)
                filled(products(out, (cst_h[:, 1, :], cst_l[:, 1, :]), (CXh[:, :, P:256], CXl[:, :, P:256]),
                                False, True))

            def mixing():
                pe.wait_ge(s_u, C["u"].at())
                for hh in range(2):
                    att_half[0] = hh
                    tiles = Tiles()
                    for m in range(4):
                        u = next_use()
                        filled(stationary(tiles, [bank(u, h, 0, HT) for h in range(2)],
                                          [half(Uh, Ul, h) for h in range(2)], KD))
                    token_major()
                    all_evacuated()
                    pe.wait_ge(s_att, C["att"].next(64 if hh == 0 else 32))
                    attention()
                token_major()
                token_major()
                fourier()

                def gates(i):
                    tiles = Tiles()
                    for pair in range(2):
                        for m in range(2):
                            blk = tiles.block(16)
                            for h in range(2):
                                u = next_use()
                                for b in range(2):
                                    for k in range(KD):
                                        wh, wl = [w[:, b * KD + k, :] for w in blk]
                                        rh, rl = half(Uh, Ul, h)(k)
                                        out = bank(u, b, 0, HT)
                                        m1 = pe.matmul(out, wh, rh, start=(k == 0), stop=False)
                                        tiles.started(m1)
                                        pe.matmul(out, wh, rl, start=False, stop=False)
                                        mm = pe.matmul(out, wl, rh, start=False, stop=(k == KD - 1))
                                filled(mm)
                        blk = tiles.block(16)
                        for m in range(2):
                            for h in range(2):
                                u = next_use()
                                for b, src in enumerate(((Yh, Yl), (Oh, Ol))):
                                    for k in range(4):
                                        wh, wl = [w[:, m * 8 + b * 4 + k, :] for w in blk]
                                        rh, rl = half(*src, h)(k)
                                        out = bank(u, b, 0, HT)
                                        m1 = pe.matmul(out, wh, rh, start=(k == 0), stop=False)
                                        tiles.started(m1)
                                        pe.matmul(out, wh, rl, start=False, stop=False)
                                        mm = pe.matmul(out, wl, rh, start=False, stop=(k == 3))
                                filled(mm)

                pe.wait_ge(s_mix, C["mix"].next())
                pairs(2, 6, 16, gates)
                pe.wait_ge(s_mrg, C["mrg"].next())
                pairs(2, 2, 4, lambda i: down(KD, Mh, Ml, 0, 4, Tiles()))
                norm()
                C["u"].next(2 * KD)

            def layer(l):
                use_no[0] = 0
                ffn()
                mixing()
                ffn()
                assert slot[0] == 0 and use_no[0] == USES

            pe.sem_inc(s_wstart, 1)
            pe.wait_ge(s_init, 3)
            pe.wait_ge(s_cst, 64)
            over_layers(pe, list(C.values()), layer)

        @block.scalar
        def _(act):
            C = make("use full func mods u32 u xc sq xn y att max cc exp pt ptc o ada kv".split())
            use = C["use"]

            def load_ada(chunk, s):
                act.dma_start(ada_w[:, s, :], a["ada"][chunk]).then_inc(s_aload[s], 16)

            def ada_pair():
                for s in (1, 0):
                    c = act.snap(C["ada"].at())
                    act.wait_ge(s_adone, c)
                    load_ada(c + 1, s)
                    C["ada"].next()

            def modulate(h, m):
                for k in range(KD):
                    act.wait_ge(s_y, C["y"].next())
                    act.wait_ge(s_u, C["u"].at() + (h * KD + k - 3))
                    for lo, hi, v in SEGS[h]:
                        i = act.activation(u32[:, k % 4, lo - h * HT:hi - h * HT], X[:, k, lo:hi], ACT.Identity,
                                           bias=m[:, v, k:k + 1], scale=m[:, v, KD + k:KD + k + 1])
                    i.then_inc(s_u32, 1)
                    C["u32"].next()

            def norm(l, s, nxt):
                for h in range(2):
                    for k in range(KD):
                        act.wait_ge(s_xc, C["xc"].next())
                        act.activation(sq[:, k, h * HT:(h + 1) * HT], X[:, k, h * HT:(h + 1) * HT],
                                       ACT.Square).then_inc(s_sq, 1)
                        C["sq"].next()
                for h in range(2):
                    act.wait_ge(s_full, C["full"].next())
                    act.activation(std[:, h, :], bank(use_no[0] + h, 1, 0, HT), ACT.Sqrt,
                                   bias=epsc[:, 0:1]).then_inc(s_func, 1)
                    C["func"].next()
                use.next(2)
                use_no[0] += 2
                act.wait_ge(s_mods, C["mods"].next())
                for h in range(2):
                    for k in range(KD):
                        act.wait_ge(s_xn, C["xn"].next())
                        act_met()
                        col = act.snap(l * (3 * KD) + (s * KD + k))
                        act.activation(X[:, k, h * HT:(h + 1) * HT], X[:, k, h * HT:(h + 1) * HT], ACT.Identity,
                                       bias=lnb[:, bass.ds(col, 1)], scale=lng[:, bass.ds(col, 1)]).then_inc(s_y, 1)
                    modulate(h, nxt)
                C["u"].next(2 * KD)

            use_no = [0]

            def skip(n):
                use.next(n)
                C["full"].next(n)
                use_no[0] += n

            def ffn(l, s):
                for size in GROUPS:
                    def up(i):
                        for _ in range(4):
                            u = use_no[0]
                            act.wait_ge(s_full, C["full"].next())
                            act.wait_ge(s_free, use.at(1))
                            act.activation(sg[:, u % 2, :], bank(u, 1, 0, HT), ACT.Silu).then_inc(s_func, 1)
                            C["func"].next()
                            use.next()
                            use_no[0] += 1
                        ada_pair()

                    start = use_no[0]
                    over(act, size // 2, [(use, 4), (C["full"], 4), (C["func"], 4), (C["ada"], 2)], up, act_met)
                    use_no[0] = start + 2 * size
                    skip(KD)
                ada_pair()
                norm(l, s, mods[(s + 1) % 3])

            def attention(hh):
                units = [(h, j) for h in range(4) for j in range(QB)] + [(h, QB) for h in range(4)]
                u0, n = use_no[0], len(units)
                for i in range(n + 2):
                    if i < n:
                        h, j = units[i]
                        act.wait_ge(s_full, C["full"].next())
                        if j < QB:
                            act.activation(pr[:, i % 3, 256:384], bank(u0 + i, 1, 384, 512), ACT.Copy)\
                                .then_inc(s_cc, 1)
                            C["cc"].next()
                        w = 384 if j < QB else P
                        act.wait_ge(s_max, C["max"].next())
                        act.activation(pr[:, i % 3, 0:w], pr[:, i % 3, 0:w], ACT.Exp, bias=stat[:, i % 4, 1:2],
                                       accum_out=stat[:, i % 4, 2:3]).then_inc(s_exp, 1)
                        C["exp"].next()
                    if 2 <= i:
                        w = 384 if units[i - 2][1] < QB else P
                        act.wait_ge(s_pt, C["pt"].next())
                        if i >= 5:
                            act.wait_ge(s_o, C["o"].next())
                        act.activation(PT[:, (i - 2) % 3, 0:w], bank(u0 + i - 2, 1, 0, w), ACT.Copy)\
                            .then_inc(s_ptc, 1)
                        C["ptc"].next()
                C["o"].next(3)
                use.next(n)
                use_no[0] += n

            def mixing(l):
                for hh in range(2):
                    if hh == 0:
                        act.wait_ge(s_gath, 16 * P)
                    act.wait_ge(s_free, use.at(-1))
                    srcs = [(G[:, :, :, :], a["gath_lh"][l * 2 + hh]), (V[:, 8, :], a["cv"][l * 2 + hh])]
                    if hh == 0:
                        srcs += [(ckT[:, :, :], a["ck"][l]), (mask[:, :, :], a["mask"])]
                    for dst, src in srcs:
                        act.dma_start(dst, src).then_inc(s_att, 16)
                        C["att"].next(16)
                    skip(4)
                    for t in range(5):
                        act.wait_ge(s_full, C["full"].next())
                        if t < 3:
                            i = act.activation(V[0:64, 4 + t, :], bank(use_no[0], 0, 0, 256, 64, 128), ACT.Copy)
                        if 0 < t < 4:
                            i = act.activation(V[64:128, 3 + t, :], bank(use_no[0], 0, 0, 256, 0, 64), ACT.Copy)
                        if t < 4:
                            i.then_inc(s_func, 1)
                            C["func"].next()
                        use.next()
                        use_no[0] += 1
                    ada_pair()
                    ada_pair()
                    act.wait_ge(s_free, use.at())
                    act.dma_start(a["new_k"][l * 2 + hh], kT[:, :, LAT:T]).then_inc(s_kv, 16)
                    act.dma_start(a["new_v"][l * 2 + hh], V[:, 7, :]).then_inc(s_kv, 16)
                    C["kv"].next(32)
                    attention(hh)
                skip(10)
                skip(14)

                def gates(i):
                    for pair in range(2):
                        for m in range(2):
                            for h in range(2):
                                u = use_no[0]
                                act.wait_ge(s_full, C["full"].next())
                                act.wait_ge(s_free, use.at(3))
                                for b in range(2):
                                    q = act.activation(sig[:, m * 2 + h, b, :], bank(u, b, 0, HT), ACT.Sigmoid)
                                q.then_inc(s_func, 1)
                                C["func"].next()
                                use.next()
                                use_no[0] += 1
                        skip(4)
                        for _ in range(1 + pair):
                            ada_pair()

                start = use_no[0]
                over(act, 2, [(use, 16), (C["full"], 16), (C["func"], 8), (C["ada"], 6)], gates, act_met)
                use_no[0] = start + 32
                over(act, 2, [(C["ada"], 2)], lambda i: ada_pair(), act_met)
                skip(KD)
                norm(l, 1, mods[2])

            def layer(l):
                use_no[0] = 0
                ffn(l, 0)
                mixing(l)
                ffn(l, 2)

            act.dma_start(craw[:, 0, :], a["c"].partition_broadcast(P)).then_inc(s_csilu, 16)
            act.dma_start(craw[:, 1, :], a["c_ctx"].partition_broadcast(P)).then_inc(s_csilu, 16)
            act.dma_start(bada[:, :], a["bada"]).then_inc(s_csilu, 16)
            for s in range(2):
                load_ada(s, s)
            act.wait_ge(s_csilu, 48)
            act.activation(csilu[:, :, :], craw[:, :, :], ACT.Silu).then_inc(s_csilu, 16)
            with act.Fori(1, ADA_SUB // 2) as i:
                for s in range(2):
                    act.wait_ge(s_adone, i * 2 + (s - 1))
                    load_ada(i * 2 + s, s)
            act.wait_ge(s_adone, ADA_SUB - 1)
            load_ada(ADA_SUB, 0)
            act.wait_ge(s_mods, 1)
            act.wait_ge(s_x, 16 * KD)
            for h in range(2):
                for k in range(KD):
                    if h * KD + k >= 4:
                        act.wait_ge(s_u, h * KD + k - 3)
                    for lo, hi, v in SEGS[h]:
                        i = act.activation(u32[:, k % 4, lo - h * HT:hi - h * HT], X[:, k, lo:hi], ACT.Identity,
                                           bias=mods[0][:, v, k:k + 1], scale=mods[0][:, v, KD + k:KD + k + 1])
                    i.then_inc(s_u32, 1)
            over_layers(act, list(C.values()), layer)
            act.wait_ge(s_kv, DEPTH * PER_LAYER["kv"])
            act.wait_ge(s_aload[0], ((1 + DEPTH * 3) * ADA_SUB // 2 + 1) * 16)

        @block.vector
        def _(dve):
            C = make("use full func h mods u32 u mean xc xn att kv max cc exp p pt o mix mrg ada dve".split())
            use = C["use"]
            use_no = [0]

            def link(i):
                i.then_inc(s_dve, 1)
                dve.wait_ge(s_dve, C["dve"].next())

            def mark(i, name):
                i.then_inc(C[name].sem, 1)
                C[name].next()

            def free(i):
                i.then_inc(s_free, 1)
                use.next()
                use_no[0] += 1

            def ada_pair(target, where, loaded, at=None):
                for s in range(2):
                    dve.wait_ge(s_aload[s], loaded)
                    link(dve.tensor_tensor_reduce(junk[:, :], ada_w[:, s, :], csilu[:, 0, :], 1.0, 0.0, ALU.mult,
                                                  ALU.add, acc4[:, 0, s:s + 1]))
                    i = dve.tensor_tensor_reduce(junk[:, :], ada_w[:, s, :], csilu[:, 1, :], 1.0, 0.0,
                                                 ALU.mult, ALU.add, acc4[:, 1, s:s + 1])
                    i.then_inc(s_adone, 1)
                    C["ada"].next()
                    dve.wait_ge(s_adone, C["ada"].at())
                link(dve.tensor_copy(target[:, :, bass.ds(where, 2)], acc4[:, :, :]))

            def finish_mods(m, q, half_gate):
                for v in range(2):
                    link(dve.tensor_tensor(m[:, v, :], m[:, v, :], bada[:, bass.ds(q * ADA_SUB, ADA_SUB)], ALU.add))
                if half_gate:
                    link(dve.tensor_scalar(m[:, :, KD:2 * KD], m[:, :, KD:2 * KD], 1.0, None, ALU.add))
                    i = dve.tensor_scalar(m[:, :, 2 * KD:], m[:, :, 2 * KD:], 0.5, None, ALU.mult)
                else:
                    i = dve.tensor_scalar(m[:, :, KD:2 * KD], m[:, :, KD:2 * KD], 1.0, None, ALU.add)
                mark(i, "mods")
                dve.wait_ge(s_mods, C["mods"].at())

            def split_u():
                for h in range(2):
                    for k in range(KD):
                        dve.wait_ge(s_u32, C["u32"].next())
                        cols = slice(h * HT, (h + 1) * HT)
                        link(dve.tensor_copy(Uh[:, k, cols], u32[:, k % 4, :]))
                        mark(dve.tensor_tensor(Ul[:, k, cols], u32[:, k % 4, :], Uh[:, k, cols].bitcast(F32),
                                               ALU.subtract), "u")

            def scale_x():
                dve.wait_ge(s_u, C["u"].at())
                link(dve.tensor_scalar(X[:, :, :], X[:, :, :], ALPHA, None, ALU.mult))

            def norm(m_next, q, half_gate):
                u = use_no[0]
                for h in range(2):
                    dve.wait_ge(s_mean, C["mean"].next())
                    for k in range(KD):
                        x = X[:, k, h * HT:(h + 1) * HT]
                        mark(dve.tensor_tensor(x, x, bank(u + h, 0, 0, HT), ALU.subtract), "xc")
                finish_mods(m_next, q, half_gate)
                for h in range(2):
                    dve.wait_ge(s_func, C["func"].next())
                    free(dve.reciprocal(std[:, h, :], std[:, h, :]))
                    dve.wait_ge(s_free, use.at())
                    C["full"].next()
                    for k in range(KD):
                        x = X[:, k, h * HT:(h + 1) * HT]
                        mark(dve.tensor_tensor(x, x, std[:, h, :], ALU.mult), "xn")
                split_u()

            def down(m, n_of, count):
                for n in range(count):
                    u = use_no[0]
                    dve.wait_ge(s_full, C["full"].next())
                    dve.wait_ge(s_free, use.at())
                    for h in range(2):
                        for lo, hi, v in SEGS[h]:
                            x = X[:, bass.ds(n_of(n), 1), lo:hi].rearrange("p a n -> p (a n)")
                            g = m[:, v, bass.ds(n_of(n) + 2 * KD, 1)]
                            i = dve.scalar_tensor_tensor(x, bank(u, h, lo - h * HT, hi - h * HT), g, x,
                                                         ALU.mult, ALU.add)
                    free(i)

            def down_loop(m):
                start = use_no[0]
                over(dve, 2, [(use, 4), (C["full"], 4)], lambda i: down(m, lambda n: i * 4 + n, 4),
                     dve_met)
                use_no[0] = start + KD

            def ffn(l, s):
                nxt = (s + 1) % 3
                scale_x()
                base = C["ada"].n
                chunk = 0
                for size in GROUPS:
                    def up(i):
                        for m in range(2):
                            for h in range(2):
                                u = use_no[0]
                                b = u % 2
                                dve.wait_ge(s_func, C["func"].next())
                                C["full"].next()
                                free(dve.tensor_tensor(hf[:, b, :], sg[:, b, :], bank(u, 0, 0, HT), ALU.mult))
                                dve.wait_ge(s_free, use.at())
                                at = bass.ds(i * 2 + m, 1)
                                hh, hl = [t[:, at, h * HT:(h + 1) * HT].rearrange("p a n -> p (a n)")
                                          for t in (Hh, Hl)]
                                link(dve.tensor_copy(hh, hf[:, b, :]))
                                mark(dve.tensor_tensor(hl, hf[:, b, :], hh.bitcast(F32), ALU.subtract), "h")
                        ada_pair(mods[nxt], i * 2 + chunk, loads(l, base + chunk, i))

                    start = use_no[0]
                    over(dve, size // 2, [(use, 4), (C["full"], 4), (C["func"], 4), (C["h"], 4), (C["ada"], 2),
                                          (C["dve"], 4 + 3)], up, dve_met)
                    use_no[0] = start + 2 * size
                    chunk += size
                    if size == 8:
                        down_loop(mods[s])
                    else:
                        down(mods[s], lambda n: n, KD)
                ada_pair(mods[nxt], chunk, loads(l, base + chunk, 0))
                norm(mods[nxt], l * 3 + (s + 1), nxt != 1)

            def loads(l, chunk, i):
                return (l * (3 * ADA_SUB) + (i * 2 + (ADA_SUB + chunk + 2))) * 8

            def attention(hh):
                units = [(h, j) for h in range(4) for j in range(QB)] + [(h, QB) for h in range(4)]
                u0, n = use_no[0], len(units)
                for i in range(n + 3):
                    if i < n:
                        h, j = units[i]
                        s3 = pr[:, i % 3, :]
                        if j == 0:
                            for kind in range(3):
                                g = G[:, h, :, BIAS_OFF[kind]:BIAS_OFF[kind] + WCOLS].rearrange("p r t -> p t r")
                                q = dve.tensor_tensor(bm[:, kind, :].rearrange("p (t r) -> p t r", r=ROWS), g,
                                                      mask[:, kind, :].rearrange("p (t r) -> p t r", r=ROWS), ALU.add)
                            link(q)
                        if i >= 3:
                            dve.wait_ge(s_pt, C["pt"].next())
                        dve.wait_ge(s_full, C["full"].next())
                        if j < QB:
                            link(dve.tensor_tensor(s3[:, 0:256], bank(u0 + i, 0, 0, 256), bm[:, BIAS_KIND[j], :],
                                                   ALU.add))
                            dve.wait_ge(s_cc, C["cc"].next())
                        else:
                            link(dve.tensor_copy(s3[:, 0:P], bank(u0 + i, 0, 0, P)))
                        w = 384 if j < QB else P
                        link(dve.tensor_reduce(stat[:, i % 4, 0:1], s3[:, 0:w], AX_X, ALU.max))
                        mark(dve.tensor_scalar(stat[:, i % 4, 1:2], stat[:, i % 4, 0:1], -1.0, None, ALU.mult), "max")
                    if 1 <= i <= n:
                        b = i - 1
                        w = 384 if units[b][1] < QB else P
                        dve.wait_ge(s_exp, C["exp"].next())
                        link(dve.reciprocal(stat[:, b % 4, 3:4], stat[:, b % 4, 2:3]))
                        mark(dve.tensor_scalar(pr[:, b % 3, 0:w], pr[:, b % 3, 0:w], stat[:, b % 4, 3:4], None,
                                               ALU.mult), "p")
                    if 3 <= i:
                        h, j = units[i - 3]
                        po, chunk = HD * (h % 2), 2 * hh + h // 2
                        dve.wait_ge(s_o, C["o"].next())
                        free(dve.tensor_copy(o32[po:po + HD, chunk, j * P:(j + 1) * P],
                                             bank(u0 + i - 3, 0, 384, 512, po, po + HD)))
                C["pt"].next(3)

            def split_from(src, hi, lo):
                link(dve.tensor_copy(hi, src))
                return dve.tensor_tensor(lo, src, hi.bitcast(F32), ALU.subtract)

            def mixing(l):
                scale_x()
                base = C["ada"].n
                chunk = 0
                for hh in range(2):
                    for m in range(4):
                        u = use_no[0]
                        dve.wait_ge(s_full, C["full"].next())
                        dst = qT if m < 2 else kT
                        for h in range(2):
                            i = dve.tensor_scalar(dst[:, m % 2, h * HT:(h + 1) * HT], bank(u, h, 0, HT),
                                                  ATTN_SCALE if m < 2 else 1.0, None, ALU.mult)
                        free(i)
                    for t in range(5):
                        u = use_no[0]
                        dve.wait_ge(s_full, C["full"].next())
                        if t < 4:
                            dve.wait_ge(s_func, C["func"].next())
                        i = dve.tensor_copy(V[:, t if t < 4 else 7, :], bank(u, 0, 0, 256))
                        free(i)
                    for _ in range(2):
                        ada_pair(mods[2], chunk, loads(l, base + chunk, 0))
                        chunk += 2
                    dve.wait_ge(s_att, C["att"].next(64 if hh == 0 else 32))
                    attention(hh)
                    dve.wait_ge(s_kv, C["kv"].next(32))
                for part in range(2):
                    for t in range(5):
                        u = use_no[0]
                        dve.wait_ge(s_full, C["full"].next())
                        cols = slice(part * 256, part * 256 + 256)
                        free(split_from(bank(u, 0, 0, 256), Fh[:, t, cols], Fl[:, t, cols]))
                for part in range(2):
                    for g in range(4):
                        u = use_no[0]
                        dve.wait_ge(s_full, C["full"].next())
                        hi, lo = ((PCh, PCl), (PSh, PSl))[part]
                        free(split_from(bank(u, 0, 0, LAT), hi[:, g, :], lo[:, g, :]))
                for g in range(4):
                    u = use_no[0]
                    dve.wait_ge(s_full, C["full"].next())
                    free(dve.tensor_copy(y32[:, g, 0:LAT], bank(u, 0, 0, LAT)))
                u = use_no[0]
                dve.wait_ge(s_full, C["full"].next())
                for b in range(2):
                    i = split_from(bank(u, b, 0, 512).rearrange("p (g n) -> p g n", g=2),
                                   CXh[:, 2 * b:2 * b + 2, :], CXl[:, 2 * b:2 * b + 2, :])
                free(i)
                u = use_no[0]
                dve.wait_ge(s_full, C["full"].next())
                free(dve.tensor_copy(y32[:, :, LAT:T], bank(u, 0, 0, LAT).rearrange("p (g n) -> p g n", g=4)))
                dve.wait_ge(s_free, use.at())
                link(dve.tensor_copy(Oh[:, :, :], o32[:, :, :]))
                link(dve.tensor_tensor(Ol[:, :, :], o32[:, :, :], Oh[:, :, :].bitcast(F32), ALU.subtract))
                link(dve.tensor_copy(Yh[:, :, :], y32[:, :, :]))
                mark(dve.tensor_tensor(Yl[:, :, :], y32[:, :, :], Yh[:, :, :].bitcast(F32), ALU.subtract), "mix")
                dve.wait_ge(s_mix, C["mix"].at())

                def gates(i):
                    for pair in range(2):
                        for _ in range(4):
                            dve.wait_ge(s_func, C["func"].next())
                            C["full"].next()
                            dve.wait_ge(s_free, use.at())
                            dve.sem_inc(s_free, 1)
                            use.next()
                            use_no[0] += 1
                        for m in range(2):
                            for h in range(2):
                                u = use_no[0]
                                s = sig[:, m * 2 + h, :, :]
                                dve.wait_ge(s_full, C["full"].next())
                                dve.tensor_tensor(ta[:, 0, :], s[:, 0, :], bank(u, 0, 0, HT), ALU.mult)
                                free(dve.tensor_tensor(ta[:, 1, :], s[:, 1, :], bank(u, 1, 0, HT), ALU.mult))
                                dve.wait_ge(s_free, use.at())
                                dst = M32[:, bass.ds(i * 4 + (pair * 2 + m), 1), h * HT:(h + 1) * HT]
                                link(dve.tensor_tensor(dst.rearrange("p a n -> p (a n)"), ta[:, 0, :], ta[:, 1, :],
                                                       ALU.add))
                        if pair == 0:
                            ada_pair(mods[2], i * 6 + chunk, loads(l, base + chunk, i * 3))
                        else:
                            for e in (2, 4):
                                ada_pair(mods[2], i * 6 + (chunk + e), loads(l, base + chunk + e, i * 3))

                start = use_no[0]
                over(dve, 2, [(use, 16), (C["full"], 16), (C["func"], 8), (C["ada"], 6), (C["dve"], 8 + 9)], gates,
                     dve_met)
                use_no[0] = start + 32
                chunk += 12
                link(dve.tensor_copy(Mh[:, :, :], M32[:, :, :]))
                mark(dve.tensor_tensor(Ml[:, :, :], M32[:, :, :], Mh[:, :, :].bitcast(F32), ALU.subtract), "mrg")
                dve.wait_ge(s_mrg, C["mrg"].at())
                over(dve, 2, [(C["ada"], 2), (C["dve"], 3)],
                     lambda i: ada_pair(mods[2], i * 2 + chunk, loads(l, base + chunk, i)), dve_met)
                down_loop(mods[1])
                norm(mods[2], l * 3 + 2, True)

            def layer(l):
                use_no[0] = 0
                ffn(l, 0)
                mixing(l)
                ffn(l, 2)

            for c in C.values():
                c.base, c.n = 0, 0
            dve.memset(epsc[:, :], LN_EPS)
            dve.memset(ones[:, :], 1.0 / D).then_inc(s_init, 1)
            dve.wait_ge(s_cst, 64)
            dve.tensor_copy(cst_h[:, :, :], cst[:, :, :]).then_inc(s_init, 1)
            dve.wait_ge(s_init, 2)
            dve.tensor_tensor(cst_l[:, :, :], cst[:, :, :], cst_h[:, :, :].bitcast(F32), ALU.subtract)\
                .then_inc(s_init, 1)
            dve.wait_ge(s_init, 3)
            dve.drain().then_inc(s_free, 4)
            dve.wait_ge(s_csilu, 64)
            over(dve, ADA_SUB // 2, [(C["ada"], 2), (C["dve"], 3)],
                 lambda i: ada_pair(mods[0], i * 2, i * 16 + 16), dve_met)
            finish_mods(mods[0], 0, True)
            split_u()
            assert C["dve"].n == FIRST_DVE, C["dve"].n
            over_layers(dve, list(C.values()), layer)


NORMS = 3 * 2 * KD
UNITS = HEADS * (QB + 1)
PER_LAYER = dict(
    tile=TILES, use=USES, full=USES, func=118, h=88, mods=3, u32=NORMS, u=NORMS, mean=6, xc=NORMS, sq=NORMS,
    xn=NORMS, y=NORMS, att=96, max=UNITS, cc=UNITS - HEADS, exp=UNITS, p=UNITS, pt=UNITS, ptc=UNITS, o=UNITS,
    mix=1, mrg=1, kv=64, ada=3 * ADA_SUB, dve=423)
FIRST_DVE = 55


def block(w, k, m):
    return w[k * P:(k + 1) * P, m * P:(m + 1) * P]


def weight_stream(w):
    deg = 2 * np.pi / LAT
    tok = (np.arange(LAT) % ROWS) * GRID_W + np.arange(LAT) // ROWS
    ang = deg * ((tok[:, None] * tok[None, :]) % LAT)
    waves = [(f(ang) / np.sqrt(LAT * P)).astype(np.float32).reshape(4, P, LAT).transpose(1, 0, 2).reshape(P, 16, P)
             for f in (np.cos, np.sin)]
    tiles = []

    def blocks(bs):
        for i in range(0, len(bs), 16):
            tiles.append(np.stack(bs[i:i + 16], axis=1))

    def ffn(up, dn):
        first = 0
        for size in GROUPS:
            for m in range(first, first + size):
                blocks([block(up, k, c) for c in (m, FF // P + m) for k in range(KD)])
            blocks([block(dn, k, n) for n in range(KD) for k in range(first, first + size)])
            first += size

    def columns(wi, lo):
        tiles.append(wi[:, lo:lo + 256].reshape(KD, P, 256).transpose(1, 0, 2).reshape(P, 16, P))

    for l in range(DEPTH):
        ffn(w["w_ff1_up"][l], w["w_ff1_down"][l])
        wi = w["w_in"][l]
        for hh in range(2):
            for c in (0, NA // P):
                blocks([block(wi, k, c + 2 * hh + m) for m in range(2) for k in range(KD)])
            columns(wi, 2 * NA + 256 * hh)
        for part in range(2):
            columns(wi, 3 * NA + 256 * part)
        tiles.extend(waves)
        c0 = 4 * NA // P
        for m in range(0, KD, 2):
            for n in (m, m + 1):
                blocks([block(wi, k, c) for c in (c0 + n, c0 + KD + n) for k in range(KD)])
            blocks([block(v[l], k, n) for n in (m, m + 1) for v in (w["w_fourier"], w["w_na_out"]) for k in range(4)])
        blocks([block(w["w_out"][l], k, n) for n in range(KD) for k in range(KD)])
        ffn(w["w_ff2_up"][l], w["w_ff2_down"][l])
    assert len(tiles) == DEPTH * TILES
    return np.stack(tiles)


def window_masks():
    out = np.zeros((P, 3, WCOLS, ROWS), np.float32)
    for kind, j in ((0, 0), (1, 1), (2, 3)):
        for c in range(QTILE):
            first = min(max(QTILE * j + c - WIN // 2, 0), GRID_W - WIN)
            for t in range(WCOLS):
                if not first <= KEY0[j] + t < first + WIN:
                    out[c * ROWS:(c + 1) * ROWS, kind, t, :] = NEG
    return out.reshape(P, 3, WCOLS * ROWS)


def small_waves():
    ang = 2 * np.pi / P * (np.outer(np.arange(P), np.arange(P)) % P)
    return np.stack([np.cos(ang), -np.sin(ang), np.cos(ang) / P, np.sin(ang) / P], axis=1).astype(np.float32)


OUTS = {"yT": (KD, P, T), "new_k": (2 * DEPTH, P, 2, P), "new_v": (2 * DEPTH, P, 256)}


def arrays_of(x):
    lat = x["x_sample"][0].reshape(ROWS, GRID_W, D).transpose(1, 0, 2).reshape(LAT, D)
    tokens = np.concatenate([lat, x["x_prompt"][0]], axis=0)
    ck = x["cache_k"][0].reshape(DEPTH, 4, 2, P, HD).transpose(0, 2, 4, 1, 3).reshape(DEPTH, P, 4, P)
    cv = x["cache_v"][0].reshape(DEPTH, 2, 4, P, HD).transpose(0, 1, 3, 2, 4).reshape(2 * DEPTH, P, 256)
    ada = x["w_ada"].transpose(0, 2, 1).reshape(DEPTH * 3 * ADA_SUB, P, D)
    bada = x["b_ada"].reshape(DEPTH * 3 * ADA_SUB, P)
    return {
        "xT": np.ascontiguousarray(tokens.T).reshape(KD, P, T),
        "c": x["c"][0], "c_ctx": x["c_ctx"],
        "wstream": weight_stream(x),
        "ada": np.concatenate([ada, np.zeros((ADA_SUB + 1, P, D), np.float32)]),
        "bada": np.ascontiguousarray(np.concatenate([bada, np.zeros((ADA_SUB, P), np.float32)]).T),
        "lng": np.ascontiguousarray(x["ln_g"].reshape(DEPTH * 3 * KD, P).T),
        "lnb": np.ascontiguousarray(x["ln_b"].reshape(DEPTH * 3 * KD, P).T),
        "rpb": np.pad(x["rpb"].reshape(DEPTH * HEADS, 2 * ROWS - 1, 2 * WIN - 1), ((0, 0), (0, 0), (16, 17))),
        "ck": np.ascontiguousarray(ck), "cv": np.ascontiguousarray(cv),
        "dft_small": small_waves(), "eye": np.eye(P, dtype=np.float32), "mask": window_masks(),
    }


def program(nc, arrays):
    a = {n: nc.dram_tensor("in_" + n, v.shape, F32, kind="ExternalInput").ap() for n, v in arrays.items()}
    for n, shape in OUTS.items():
        a[n] = nc.dram_tensor(n, shape, F32, kind="ExternalOutput").ap()
    a["gath"] = nc.dram_tensor("gath", (DEPTH * HEADS, P, ROWS, TW), F32, kind="Internal").ap()
    a["gath_lh"] = a["gath"].rearrange("(q h) p r t -> q p h r t", h=4)
    build(nc, a)


def outputs_of(r):
    y = np.asarray(r["yT"]).reshape(D, T).T
    y_s = y[:LAT].reshape(GRID_W, ROWS, D).transpose(1, 0, 2).reshape(1, LAT, D)
    y_p = y[LAT:].reshape(1, CTX, D)
    nk = np.asarray(r["new_k"]).reshape(DEPTH, 2, 2, HD, 2, P).transpose(0, 1, 4, 2, 5, 3)
    nv = np.asarray(r["new_v"]).reshape(DEPTH, 2, P, 4, HD).transpose(0, 1, 3, 2, 4)
    shape = (1, DEPTH, HEADS, P, HD)
    return tuple(np.ascontiguousarray(v) for v in (y_p, y_s, nk.reshape(shape), nv.reshape(shape)))


def kernel(**inputs):
    import concourse.bacc as _bacc
    from concourse.bass_utils import run_bass_kernel_spmd as _run

    arrays = arrays_of({n: np.asarray(v) for n, v in inputs.items()})
    arrays = {n: np.ascontiguousarray(v) for n, v in arrays.items()}
    nc = _bacc.Bacc("TRN2", target_bir_lowering=False, num_devices=1)
    program(nc, arrays)
    r = _run(nc, [{"in_" + n: v for n, v in arrays.items()}], core_ids=[0])
    return outputs_of(r.results[0])
```

```python
import numpy as np
from contextlib import ExitStack

import concourse.bass as bass
import concourse.mybir as mybir

F32 = mybir.dt.float32
F32R = mybir.dt.float32r
BF16 = mybir.dt.bfloat16
ALU = mybir.AluOpType
ACT = mybir.ActivationFunctionType
AX_X = mybir.AxisListType.X

P = 128
D = 1024
KD = D // P
DEPTH = 2
LAT, CTX = 512, 128
T = LAT + CTX
HT = T // 2
FF = 2816
HEADS, HD = 8, 64
NA = HEADS * HD
GRID_W, ROWS = 64, LAT // 64
WIN = 16
ATTN_SCALE = HD ** -0.5
ALPHA = (2 * DEPTH) ** 0.25
LN_EPS = 1e-5
NEG = -1e30

GROUPS = (8, 8, 6)
QTILE = 16
QB = GRID_W // QTILE
WCOLS = 32
KEY0 = (0, 8, 24, 32)
VTILES = ((0, 1), (4, 5), (5, 6), (2, 3))
BIAS_KIND = (0, 1, 1, 2)
BIAS_OFF = (16, 8, 0)
TW = 48
RW = 64
SEGS = (((0, HT, 0),), ((HT, LAT, 0), (LAT, T, 1)))

ADA_SUB = 3 * KD
TILES = 102
USES = 264

FIRST_ADA = 2 * KD


class Count:

    def __init__(self, sem, per_layer, first=0):
        self.sem, self.per_layer, self.first = sem, per_layer, first
        self.base, self.n = first, 0

    def at(self, back=0):
        return self.base + (self.n - back)

    def next(self, k=1):
        self.n += k
        return self.at()


def over(eng, trips, steps, body, met):
    met()
    kept = [(c, c.base, c.n) for c, _ in steps]
    with eng.Fori(0, trips) as i:
        for c, s in steps:
            c.base, c.n = eng.snap(c.at() + i * s), 0
        body(i)
        for c, s in steps:
            assert c.n == s, (c.sem, c.n, s)
    for (c, base, n), (_, s) in zip(kept, steps):
        c.base, c.n = base, n + trips * s


def over_layers(eng, counts, body):
    with eng.Fori(0, DEPTH) as layer:
        for c in counts:
            c.base, c.n = eng.snap(layer * c.per_layer + c.first), 0
        body(layer)
        for c in counts:
            assert c.n == c.per_layer, (c.sem, c.n, c.per_layer)
    for c in counts:
        c.base, c.n = c.first + DEPTH * c.per_layer, 0


def build(nc, a):
    ctx = ExitStack()
    with ctx:
        def sb(name, shape, dt=F32):
            return ctx.enter_context(nc.sbuf_tensor(name, shape, dt))

        def sem(name):
            return ctx.enter_context(nc.semaphore(name))

        X = sb("X", [P, KD, T])
        Uh = sb("Uh", [P, KD, T], F32R)
        Ul = sb("Ul", [P, KD, T], F32R)
        w_raw = sb("w_raw", [P, 2, 16, P])
        w_hi = sb("w_hi", [P, 2, 16, P], F32R)
        w_lo = sb("w_lo", [P, 2, 16, P], F32R)
        ada_w = sb("ada_w", [P, 2, D])
        junk = sb("junk", [P, D], BF16)
        csilu = sb("csilu", [P, 2, D])
        cst_h = sb("cst_h", [P, 4, P], F32R)
        cst_l = sb("cst_l", [P, 4, P], F32R)
        ident = sb("ident", [P, P])
        ones = sb("ones", [P, P])
        lng = sb("lng", [P, DEPTH * 3 * KD])
        lnb = sb("lnb", [P, DEPTH * 3 * KD])
        lng0 = sb("lng0", [P, DEPTH * 3 * KD])
        lnb0 = sb("lnb0", [P, DEPTH * 3 * KD])
        bada = sb("bada", [P, (1 + DEPTH * 3) * ADA_SUB])
        mods = [sb(f"mods{s}", [P, 2, ADA_SUB]) for s in range(3)]
        acc4 = sb("acc4", [P, 2, 2])
        lnm = sb("lnm", [P, 2, 2, KD])
        epsc = sb("epsc", [P, 1])
        zone_bytes = 75776
        z0 = -(-nc.sbuf_base // 32) * 32
        sb("zone", [P, zone_bytes // 4 + 8])

        def at(name, off, shape, dt=F32):
            size = 4 * int(np.prod(shape[1:]))
            assert off + size <= zone_bytes, (name, off + size)
            return nc.alloc_sbuf_tensor_at(name, shape, dt, offset=z0 + off)

        Hh = at("Hh", 0, [P, 8, T], F32R)
        Hl = at("Hl", 20480, [P, 8, T], F32R)
        sg = at("sg", 40960, [P, 2, HT])
        hf = at("hf", 43520, [P, 2, HT])
        norm_mem = {}
        for where, offs in (("f", (46080, 48640, 53760, 58880, 61440)), ("m", (5120, 7680, 12800, 17920, 61440))):
            norm_mem[where] = (at("std_" + where, offs[0], [P, 2, HT]), at("u32_" + where, offs[1], [P, 4, HT]),
                               at("sq_" + where, offs[2], [P, 4, HT]), at("sum_" + where, offs[3], [P, 2, HT]),
                               at("sqsum_" + where, offs[4], [P, 2, HT]))
        craw = at("craw", 0, [P, 2, D])
        cst = at("cst", 8192, [P, 4, P])
        ada0 = at("ada0", 10240, [P, FIRST_ADA, D])
        o32 = at("o32", 0, [P, 4, T])
        y32 = at("y32", 10240, [P, 4, T])
        qT = at("qT", 20480, [P, 2, T])
        kT = at("kT", 25600, [P, 2, T])
        ckT = at("ckT", 30720, [P, 4, P])
        V = at("V", 32768, [P, 9, 256])
        G = at("G", 41984, [P, 4, ROWS, TW])
        mask = at("mask", 48128, [P, 3, 256])
        bm = at("bm", 51200, [P, 3, 256])
        pr = at("pr", 54272, [P, 3, 384])
        PT = at("PT", 58880, [P, 3, 384])
        stat = at("stat", 63488, [P, 4, 4])
        Fh = at("Fh", 20480, [P, 5, NA], F32R)
        Fl = at("Fl", 30720, [P, 5, NA], F32R)
        PCh = at("PCh", 40960, [P, 4, LAT], F32R)
        PCl = at("PCl", 49152, [P, 4, LAT], F32R)
        PSh = at("PSh", 57344, [P, 4, LAT], F32R)
        PSl = at("PSl", 65536, [P, 4, LAT], F32R)
        CXh = at("CXh", 57344, [P, 4, 256], F32R)
        CXl = at("CXl", 61440, [P, 4, 256], F32R)
        Oh = at("Oh", 20480, [P, 4, T], F32R)
        Ol = at("Ol", 30720, [P, 4, T], F32R)
        Yh = at("Yh", 40960, [P, 4, T], F32R)
        Yl = at("Yl", 51200, [P, 4, T], F32R)
        sig = at("sig", 61440, [P, 4, 2, HT])
        ta = at("ta", 71680, [P, 2, HT])
        M32 = at("M32", 0, [P, KD, T])
        Mh = at("Mh", 20480, [P, KD, T], F32R)
        Ml = at("Ml", 40960, [P, KD, T], F32R)

        psum = ctx.enter_context(nc.psum_tensor("psum", [P, 8, 512], F32))

        def bank(u, b, lo, hi, p0=0, p1=P):
            return psum[p0:p1, 2 * (u % 4) + b, lo:hi]

        s_x = sem("x_loaded")
        s_cst = sem("const_loaded")
        s_gath = sem("bias_gathered")
        s_wload = [sem(f"w_loaded{s}") for s in range(2)]
        s_whi = sem("w_hi_done")
        s_wsplit = sem("w_split")
        s_wstart = sem("w_tile_started")
        s_aload = [sem(f"ada_loaded{s}") for s in range(2)]
        s_adone = sem("ada_chunk_done")
        s_ada0 = [sem(f"first_ada_loaded{s}") for s in range(4)]
        s_csilu = sem("csilu_done")
        s_init = sem("constants_ready")
        s_full = sem("psum_full")
        s_free = sem("psum_free")
        s_func = sem("function_done")
        s_h = sem("hidden_ready")
        s_dve = sem("vector_step")
        s_mods = sem("mods_ready")
        s_u32 = sem("modulated")
        s_u = sem("u_ready")
        s_mean = sem("mean_ready")
        s_xc = sem("centred")
        s_sq = sem("squared")
        s_sum = sem("sum_ready")
        s_added = sem("square_added")
        s_sqsum = sem("square_sum_ready")
        s_var = sem("variance_ready")
        s_std = sem("deviation_ready")
        s_xn = sem("normed")
        s_y = sem("post_norm_done")
        s_att = sem("attention_inputs")
        s_max = sem("max_ready")
        s_cc = sem("cached_scores_copied")
        s_exp = sem("exp_done")
        s_o = sem("head_output_ready")
        s_p = sem("probs_ready")
        s_pt = sem("probs_transposed")
        s_ptc = sem("probs_copied")
        s_mix = sem("branch_inputs_split")
        s_mrg = sem("merged_split")
        s_kv = sem("kv_stored")
        s_out = sem("y_stored")

        def pool_met(s):
            nc.gpsimd.sem_inc(s_stands["pool"], 1)

        def pe_met():
            nc.tensor.sem_inc(s_stands["pe"], 1)

        def act_met():
            nc.scalar.sem_inc(s_stands["act"], 1)

        def dve_met():
            nc.vector.sem_inc(s_stands["dve"], 1)

        s_stands = {e: sem("wait_taken_" + e) for e in ("pool", "pe", "act", "dve")}
        block = ctx.enter_context(nc.Block())

        def make(which, **other):
            per = dict(PER_LAYER)
            sems = dict(
                tile=s_wstart, use=s_free, full=s_full, func=s_func, h=s_h, mods=s_mods, u32=s_u32,
                sum=s_sum, added=s_added, sqsum=s_sqsum, var=s_var, std=s_std, u=s_u, mean=s_mean, xc=s_xc, sq=s_sq, xn=s_xn, y=s_y, att=s_att, max=s_max,
                cc=s_cc, exp=s_exp, p=s_p, pt=s_pt, ptc=s_ptc, o=s_o, mix=s_mix, mrg=s_mrg,
                kv=s_kv, ada=s_adone, dve=s_dve)
            first = dict(use=4, tile=1, ada=1, mods=1, u=2 * KD, u32=2 * KD, dve=FIRST_DVE) | other
            return {k: Count(sems[k], per[k], first.get(k, 0)) for k in which}

        @block.sync
        def _(sp):
            for q in range(4):
                n = FIRST_ADA // 4
                sp.dma_start(ada0[:, q * n:(q + 1) * n, :],
                             a["ada"][q * n:(q + 1) * n].rearrange("c p k -> p c k")).then_inc(s_ada0[q], 16)
            for k in range(KD):
                sp.dma_start(X[:, k, :], a["xT"][k]).then_inc(s_x, 16)
            sp.dma_start(cst[:, :, :], a["dft_small"]).then_inc(s_cst, 16)
            sp.dma_start(ident[:, :], a["eye"]).then_inc(s_cst, 16)
            sp.dma_start(lng[:, :], a["lng"]).then_inc(s_cst, 16)
            sp.dma_start(lnb[:, :], a["lnb"]).then_inc(s_cst, 16)
            for s in range(2):
                sp.dma_start(w_raw[:, s, :, :], a["wstream"][s]).then_inc(s_wload[s], 16)
            for c in range(QTILE):
                for r in range(ROWS):
                    src = a["rpb"][:, ROWS - 1 - r:2 * ROWS - 1 - r, QTILE - 1 - c:QTILE - 1 - c + TW]
                    sp.dma_start(a["gath"][:, c * ROWS + r, :, :], src).then_inc(s_gath, 16)
            with sp.Fori(1, DEPTH * TILES // 2) as j:
                for s in range(2):
                    sp.wait_ge(s_wsplit, j * 2 + (s - 1))
                    sp.dma_start(w_raw[:, s, :, :], a["wstream"][j * 2 + s]).then_inc(s_wload[s], 16)
            sp.wait_ge(s_y, DEPTH * PER_LAYER["y"])
            for k in range(KD):
                sp.dma_start(a["yT"][k], X[:, k, :]).then_inc(s_out, 16)
            sp.wait_ge(s_out, 16 * KD)

        @block.gpsimd
        def _(pool):
            with pool.Fori(0, DEPTH * TILES // 2) as j:
                for s in range(2):
                    pool.wait_ge(s_wload[s], j * 16 + 16)
                    pool.wait_ge(s_wstart, j * 2 + (s + 1))
                    pool_met(s)
                    pool.tensor_scalar(w_hi[:, s, :, :], w_raw[:, s, :, :], 1.0, 0.0, ALU.mult,
                                       ALU.add).then_inc(s_whi, 1)
                    pool.wait_ge(s_whi, j * 2 + (s + 1))
                    pool.tensor_tensor(w_lo[:, s, :, :], w_raw[:, s, :, :],
                                       w_hi[:, s, :, :].bitcast(F32), ALU.subtract).then_inc(s_wsplit, 1)

        @block.tensor
        def _(pe):
            C = make("tile use full h u mean sum sqsum var att p pt ptc o mix mrg".split(), u=0)
            tile, use = C["tile"], C["use"]
            slot = [0]

            def products(out, left, right, first, last):
                (lh, ll), (rh, rl) = left, right
                pe.matmul(out, lh, rh, start=first, stop=False)
                pe.matmul(out, lh, rl, start=False, stop=False)
                return pe.matmul(out, ll, rh, start=False, stop=last)

            class Tiles:

                def __init__(self):
                    self.left = 0

                def block(self, n=1, as_moving=False):
                    if self.left == 0:
                        pe.wait_ge(s_wsplit, tile.at())
                        self.left, self.fresh = 16, True
                        self.s = slot[0]
                        slot[0] ^= 1
                    b = 16 - self.left
                    self.left -= n
                    view = [w[:, self.s, b:b + n, :] for w in (w_hi, w_lo)]
                    return view

                def started(self, mm):
                    if self.fresh:
                        mm.then_inc(s_wstart, 1)
                        tile.next()
                        self.fresh = False

            use_no = [0]

            def next_use():
                pe.wait_ge(s_free, use.at(3))
                use.next()
                use_no[0] += 1
                return use_no[0] - 1

            def all_evacuated():
                pe.wait_ge(s_free, use.at())

            def filled(mm):
                mm.then_inc(s_full, 1)
                C["full"].next()

            def stationary(tiles, outs, moving, nk):
                for k in range(nk):
                    wh, wl = tiles.block()
                    wh, wl = wh[:, 0, :], wl[:, 0, :]
                    for i, (out, mv) in enumerate(zip(outs, moving)):
                        rh, rl = mv(k)
                        m1 = pe.matmul(out, wh, rh, start=(k == 0), stop=False)
                        tiles.started(m1)
                        pe.matmul(out, wh, rl, start=False, stop=False)
                        mm = pe.matmul(out, wl, rh, start=False, stop=(k == nk - 1))
                return mm

            def half(th, tl, h):
                return lambda k: (th[:, k, h * HT:(h + 1) * HT], tl[:, k, h * HT:(h + 1) * HT])

            def mean_of(u):
                pe.wait_ge(s_sum, C["sum"].next())
                h = halves["sum"]
                pe.matmul(bank(u, 0, 0, HT), ones[:, :], halves["mem"][3][:, h, :], start=True,
                          stop=True).then_inc(s_mean, 1)
                C["mean"].next()

            def variance_of(u):
                pe.wait_ge(s_sqsum, C["sqsum"].next())
                h = halves["sum"]
                pe.matmul(bank(u, 1, 0, HT), ones[:, :], halves["mem"][4][:, h, :], start=True,
                          stop=True).then_inc(s_var, 1)
                C["var"].next()
                halves["sum"] = 1 - h

            halves = {"sum": 0, "mem": None}

            def down_halves(nk, mh, ml, mem):
                halves["mem"] = mem
                for h in range(2):
                    tiles = Tiles()
                    if h == 1:
                        un = next_use()
                    mv = half(mh, ml, h)
                    for pair in range(KD // 2):
                        u = next_use()
                        for b in range(2):
                            mm = stationary(tiles, [bank(u, b, 0, HT)], [mv], nk)
                            if h == 1 and (pair, b) == (0, 0):
                                mean_of(un)
                            if h == 1 and (pair, b) == (2, 0):
                                variance_of(un)
                        filled(mm)

            def down(nk, mh, ml, n0, n1, tiles):
                for n in range(n0, n1):
                    u = next_use()
                    mm = stationary(tiles, [bank(u, h, 0, HT) for h in range(2)],
                                    [half(mh, ml, h) for h in range(2)], nk)
                    filled(mm)

            def pairs(trips, tiles_per, uses_per, body, extra=()):
                assert tiles_per % 2 == 0 and uses_per % 4 == 0
                start = use_no[0]
                over(pe, trips, [(tile, tiles_per), (use, uses_per), (C["full"], uses_per)]
                     + list(extra), body, pe_met)
                use_no[0] = start + uses_per * trips

            def u_ready(h, k):
                pe.wait_ge(s_u, C["u"].at() + (h * KD + k + 1))

            def first_up(pending):
                tiles = Tiles()
                un = next_use() if pending else None
                pairs_ = []
                for m in range(2):
                    pairs_.append(tiles.block(16))
                    u = next_use()
                    for b in range(2):
                        for k in range(KD):
                            if m == 0 and b == 0:
                                u_ready(0, k)
                            wh, wl = [w[:, b * KD + k, :] for w in pairs_[m]]
                            rh, rl = half(Uh, Ul, 0)(k)
                            out = bank(u, b, 0, HT)
                            m1 = pe.matmul(out, wh, rh, start=(k == 0), stop=False)
                            if m == 0:
                                tiles.started(m1)
                            pe.matmul(out, wh, rl, start=False, stop=False)
                            mm = pe.matmul(out, wl, rh, start=False, stop=(k == KD - 1))
                        if pending and (m, b) == (0, 1):
                            filled(mm)
                            mean_of(un)
                    if not (pending and m == 0):
                        filled(mm)
                if pending:
                    variance_of(un)
                for m in range(2):
                    u = next_use()
                    for k in range(KD):
                        if m == 0:
                            u_ready(1, k)
                        for b in range(2):
                            wh, wl = [w[:, b * KD + k, :] for w in pairs_[m]]
                            rh, rl = half(Uh, Ul, 1)(k)
                            out = bank(u, b, 0, HT)
                            m1 = pe.matmul(out, wh, rh, start=(k == 0), stop=False)
                            if m == 1:
                                tiles.started(m1)
                            pe.matmul(out, wh, rl, start=False, stop=False)
                            mm = pe.matmul(out, wl, rh, start=False, stop=(k == KD - 1))
                    filled(mm)
                C["u"].next(2 * KD)

            def ffn(pending):
                first_up(pending)
                for group, size in enumerate(GROUPS):
                    def up(i):
                        tiles = Tiles()
                        for m in range(2):
                            pair = tiles.block(16)
                            for h in range(2):
                                u = next_use()
                                for b in range(2):
                                    for k in range(KD):
                                        wh, wl = [w[:, b * KD + k, :] for w in pair]
                                        rh, rl = half(Uh, Ul, h)(k)
                                        out = bank(u, b, 0, HT)
                                        m1 = pe.matmul(out, wh, rh, start=(k == 0), stop=False)
                                        tiles.started(m1)
                                        pe.matmul(out, wh, rl, start=False, stop=False)
                                        mm = pe.matmul(out, wl, rh, start=False, stop=(k == KD - 1))
                                filled(mm)

                    pairs(size // 2 - (group == 0), 2, 4, up)
                    pe.wait_ge(s_h, C["h"].next(2 * size))
                    if group < 2:
                        pairs(2, 2, 4, lambda i: down(8, Hh, Hl, 0, 4, Tiles()))
                down_halves(size, Hh, Hl, norm_mem["f"])

            def attention():
                units = [(h, j) for h in range(4) for j in range(QB)] + [(h, QB) for h in range(4)]
                u0 = use_no[0]
                n = len(units)
                for i in range(n + 3):
                    if i < n:
                        h, j = units[i]
                        u = next_use()
                        po, hp = HD * (h % 2), h // 2
                        if j < QB:
                            q = qT[po:po + HD, hp, j * P:(j + 1) * P]
                            pe.matmul(bank(u, 0, 0, 256), q,
                                      kT[po:po + HD, hp, KEY0[j] * ROWS:KEY0[j] * ROWS + 256],
                                      start=True, stop=True)
                            mm = pe.matmul(bank(u, 1, 384, 512), q,
                                           ckT[po:po + HD, 2 * att_half[0] + hp, :], start=True, stop=True)
                        else:
                            mm = pe.matmul(bank(u, 0, 0, P), qT[po:po + HD, hp, LAT:T],
                                           kT[po:po + HD, hp, LAT:T], start=True, stop=True)
                        filled(mm)
                    if 2 <= i < n + 2:
                        h, j = units[i - 2]
                        u = u0 + i - 2
                        pe.wait_ge(s_p, C["p"].next())
                        for t in range(3 if j < QB else 1):
                            mm = pe.transpose(bank(u, 1, t * P, (t + 1) * P), pr[:, (i - 2) % 3, t * P:(t + 1) * P],
                                              ident[:, :])
                        mm.then_inc(s_pt, 1)
                        C["pt"].next()
                    if 3 <= i:
                        h, j = units[i - 3]
                        u = u0 + i - 3
                        po = HD * (h % 2)
                        pe.wait_ge(s_ptc, C["ptc"].next())
                        vt = VTILES[j] + (8,) if j < QB else (7,)
                        for t, v in enumerate(vt):
                            mm = pe.matmul(bank(u, 0, 384, 512, po, po + HD), V[:, v, h * HD:(h + 1) * HD],
                                           PT[:, (i - 3) % 3, t * P:(t + 1) * P],
                                           start=(t == 0), stop=(t == len(vt) - 1))
                        mm.then_inc(s_o, 1)
                        C["o"].next()

            att_half = [0]

            def token_major():
                wh, wl = [w.rearrange("p (k c) n -> p k (c n)", k=KD) for w in vf_tiles.block(16)]
                for t in range(T // P):
                    u = next_use()
                    for k in range(KD):
                        uh, ul = Uh[:, k, t * P:(t + 1) * P], Ul[:, k, t * P:(t + 1) * P]
                        out = bank(u, 0, 0, 256)
                        m1 = pe.matmul(out, uh, wh[:, k, :], start=(k == 0), stop=False)
                        vf_tiles.started(m1)
                        pe.matmul(out, uh, wl[:, k, :], start=False, stop=False)
                        mm = pe.matmul(out, ul, wh[:, k, :], start=False, stop=(k == KD - 1))
                    filled(mm)

            vf_tiles = Tiles()

            def fourier():
                for part in range(2):
                    wh, wl = [w.rearrange("p (k c) n -> p k (c n)", k=4) for w in vf_tiles.block(16)]
                    if part == 0:
                        all_evacuated()
                    for g in range(4):
                        u = next_use()
                        for kt in range(4):
                            fh, fl = [f[:, kt, g * P:(g + 1) * P] for f in (Fh, Fl)]
                            out = bank(u, 0, 0, LAT)
                            m1 = pe.matmul(out, fh, wh[:, kt, :], start=(kt == 0), stop=False)
                            vf_tiles.started(m1)
                            pe.matmul(out, fh, wl[:, kt, :], start=False, stop=False)
                            mm = pe.matmul(out, fl, wh[:, kt, :], start=False, stop=(kt == 3))
                        filled(mm)
                for g in range(4):
                    if g == 0:
                        all_evacuated()
                    u = next_use()
                    out = bank(u, 0, 0, LAT)
                    products(out, (cst_h[:, 0, :], cst_l[:, 0, :]), (PCh[:, g, :], PCl[:, g, :]), True, False)
                    filled(products(out, (cst_h[:, 1, :], cst_l[:, 1, :]), (PSh[:, g, :], PSl[:, g, :]),
                                    False, True))
                u = next_use()
                ch, cl = [c[:, 2:4, :] for c in (cst_h, cst_l)]
                for g in range(4):
                    fh, fl = [f[:, 4, g * P:(g + 1) * P] for f in (Fh, Fl)]
                    mm = products(bank(u, g // 2, 256 * (g % 2), 256 * (g % 2) + 256), (fh, fl), (ch, cl), True, True)
                filled(mm)
                all_evacuated()
                u = next_use()
                out = bank(u, 0, 0, LAT).rearrange("p (g n) -> p g n", g=4)
                products(out, (cst_h[:, 0, :], cst_l[:, 0, :]), (CXh[:, :, 0:P], CXl[:, :, 0:P]), True, False)
                filled(products(out, (cst_h[:, 1, :], cst_l[:, 1, :]), (CXh[:, :, P:256], CXl[:, :, P:256]),
                                False, True))

            def mixing():
                tiles = Tiles()
                un = next_use()
                us, blks = [], []
                for m in range(3):
                    blks.append([tiles.block() for _ in range(KD)])
                    us.append(next_use())
                    for k in range(KD):
                        if m == 0:
                            u_ready(0, k)
                        wh, wl = [w[:, 0, :] for w in blks[m][k]]
                        rh, rl = half(Uh, Ul, 0)(k)
                        out = bank(us[m], 0, 0, HT)
                        m1 = pe.matmul(out, wh, rh, start=(k == 0), stop=False)
                        if m < 2:
                            tiles.started(m1)
                        pe.matmul(out, wh, rl, start=False, stop=False)
                        pe.matmul(out, wl, rh, start=False, stop=(k == KD - 1))
                    if m == 0:
                        mean_of(un)
                variance_of(un)
                for m in range(3):
                    for k in range(KD):
                        if m == 0:
                            u_ready(1, k)
                        wh, wl = [w[:, 0, :] for w in blks[m][k]]
                        rh, rl = half(Uh, Ul, 1)(k)
                        out = bank(us[m], 1, 0, HT)
                        m1 = pe.matmul(out, wh, rh, start=(k == 0), stop=False)
                        if m == 2:
                            tiles.started(m1)
                        pe.matmul(out, wh, rl, start=False, stop=False)
                        mm = pe.matmul(out, wl, rh, start=False, stop=(k == KD - 1))
                    filled(mm)
                C["u"].next(2 * KD)
                for hh in range(2):
                    att_half[0] = hh
                    if hh == 1:
                        tiles = Tiles()
                    for m in range(3 if hh == 0 else 0, 4):
                        u = next_use()
                        filled(stationary(tiles, [bank(u, h, 0, HT) for h in range(2)],
                                          [half(Uh, Ul, h) for h in range(2)], KD))
                    token_major()
                    all_evacuated()
                    pe.wait_ge(s_att, C["att"].next(64 if hh == 0 else 32))
                    attention()
                token_major()
                token_major()
                fourier()

                def gates(i):
                    tiles = Tiles()
                    for pair in range(2):
                        for m in range(2):
                            blk = tiles.block(16)
                            for h in range(2):
                                u = next_use()
                                for b in range(2):
                                    for k in range(KD):
                                        wh, wl = [w[:, b * KD + k, :] for w in blk]
                                        rh, rl = half(Uh, Ul, h)(k)
                                        out = bank(u, b, 0, HT)
                                        m1 = pe.matmul(out, wh, rh, start=(k == 0), stop=False)
                                        tiles.started(m1)
                                        pe.matmul(out, wh, rl, start=False, stop=False)
                                        mm = pe.matmul(out, wl, rh, start=False, stop=(k == KD - 1))
                                filled(mm)
                        blk = tiles.block(16)
                        for m in range(2):
                            for h in range(2):
                                u = next_use()
                                for b, src in enumerate(((Yh, Yl), (Oh, Ol))):
                                    for k in range(4):
                                        wh, wl = [w[:, m * 8 + b * 4 + k, :] for w in blk]
                                        rh, rl = half(*src, h)(k)
                                        out = bank(u, b, 0, HT)
                                        m1 = pe.matmul(out, wh, rh, start=(k == 0), stop=False)
                                        tiles.started(m1)
                                        pe.matmul(out, wh, rl, start=False, stop=False)
                                        mm = pe.matmul(out, wl, rh, start=False, stop=(k == 3))
                                filled(mm)

                pe.wait_ge(s_mix, C["mix"].next())
                pairs(2, 6, 16, gates)
                pe.wait_ge(s_mrg, C["mrg"].next())
                down_halves(KD, Mh, Ml, norm_mem["m"])

            def layer(l):
                use_no[0] = 0
                ffn(False)
                mixing()
                ffn(True)
                un = next_use()
                mean_of(un)
                variance_of(un)
                assert slot[0] == 0 and use_no[0] == USES

            pe.sem_inc(s_wstart, 1)
            pe.wait_ge(s_init, 3)
            pe.wait_ge(s_cst, 64)
            over_layers(pe, list(C.values()), layer)

        @block.scalar
        def _(act):
            C = make("use full func mods u32 u xc sq added var std xn y att max cc exp pt ptc o ada kv".split())
            use = C["use"]

            def load_ada(chunk, s):
                act.dma_start(ada_w[:, s, :], a["ada"][chunk]).then_inc(s_aload[s], 16)

            def ada_pair():
                for s in (1, 0):
                    c = act.snap(C["ada"].at())
                    act.wait_ge(s_adone, c)
                    load_ada(c + FIRST_ADA, s)
                    C["ada"].next()

            def squares(h):
                for k in range(KD):
                    act.wait_ge(s_xc, C["xc"].next())
                    if k >= 4:
                        act.wait_ge(s_added, C["added"].next())
                    act.activation(sq[:, k % 4, :], X[:, k, h * HT:(h + 1) * HT], ACT.Square).then_inc(s_sq, 1)
                    C["sq"].next()
                C["added"].next(2)

            def deviation(u, h):
                act.wait_ge(s_var, C["var"].next())
                act.activation(std[:, h, :], bank(u, 1, 0, HT), ACT.Sqrt, bias=epsc[:, 0:1]).then_inc(s_std, 1)
                C["std"].next()
                use.next()
                use_no[0] += 1

            def finish(l, s, h):
                for k in range(KD):
                    act.wait_ge(s_xn, C["xn"].next())
                    act.wait_ge(s_u, C["u"].at() + (h * KD + k - 3))
                    for lo, hi, v in SEGS[h]:
                        i = act.activation(u32[:, k % 4, lo - h * HT:hi - h * HT], X[:, k, lo:hi], ACT.Identity,
                                           bias=lnm[:, v, 1, k:k + 1], scale=lnm[:, v, 0, k:k + 1])
                    i.then_inc(s_u32, 1)
                    C["u32"].next()
                    act.wait_ge(s_u32, C["u32"].at())
                    act_met()
                    col = act.snap(l * (3 * KD) + (s * KD + k))
                    act.activation(X[:, k, h * HT:(h + 1) * HT], X[:, k, h * HT:(h + 1) * HT], ACT.Identity,
                                   bias=lnb[:, bass.ds(col, 1)], scale=lng[:, bass.ds(col, 1)]).then_inc(s_y, 1)
                    C["y"].next()
                if h == 1:
                    C["u"].next(2 * KD)

            def norm(l, s, h, mem):
                nonlocal std, u32, sq
                std, u32, sq = mem[:3]
                u = use_no[0]
                squares(h)
                deviation(u, h)
                if h == 0:
                    act.wait_ge(s_mods, C["mods"].next())
                finish(l, s, h)

            def last_products(l, s, mem):
                skip(KD // 2)
                norm(l, s, 0, mem)
                skip(KD // 2)

            std = u32 = sq = None

            use_no = [0]

            def skip(n):
                use.next(n)
                C["full"].next(n)
                use_no[0] += n

            def ffn(l, s, pending):
                if pending:
                    norm(l, s - 1, 1, norm_mem["m"])
                for group, size in enumerate(GROUPS):
                    def up(i):
                        for _ in range(4):
                            u = use_no[0]
                            act.wait_ge(s_full, C["full"].next())
                            act.wait_ge(s_free, use.at(1))
                            act.activation(sg[:, u % 2, :], bank(u, 1, 0, HT), ACT.Silu).then_inc(s_func, 1)
                            C["func"].next()
                            use.next()
                            use_no[0] += 1
                        ada_pair()

                    if group == 0:
                        up(0)
                    start = use_no[0]
                    n = size // 2 - (group == 0)
                    over(act, n, [(use, 4), (C["full"], 4), (C["func"], 4), (C["ada"], 2)], up, act_met)
                    use_no[0] = start + 4 * n
                    if group < 2:
                        skip(KD)
                ada_pair()
                last_products(l, s, norm_mem["f"])

            def attention(hh):
                units = [(h, j) for h in range(4) for j in range(QB)] + [(h, QB) for h in range(4)]
                u0, n = use_no[0], len(units)
                for i in range(n + 2):
                    if i < n:
                        h, j = units[i]
                        act.wait_ge(s_full, C["full"].next())
                        if j < QB:
                            act.activation(pr[:, i % 3, 256:384], bank(u0 + i, 1, 384, 512), ACT.Copy)\
                                .then_inc(s_cc, 1)
                            C["cc"].next()
                        w = 384 if j < QB else P
                        act.wait_ge(s_max, C["max"].next())
                        act.activation(pr[:, i % 3, 0:w], pr[:, i % 3, 0:w], ACT.Exp, bias=stat[:, i % 4, 1:2],
                                       accum_out=stat[:, i % 4, 2:3]).then_inc(s_exp, 1)
                        C["exp"].next()
                    if 2 <= i:
                        w = 384 if units[i - 2][1] < QB else P
                        act.wait_ge(s_pt, C["pt"].next())
                        if i >= 5:
                            act.wait_ge(s_o, C["o"].next())
                        act.activation(PT[:, (i - 2) % 3, 0:w], bank(u0 + i - 2, 1, 0, w), ACT.Copy)\
                            .then_inc(s_ptc, 1)
                        C["ptc"].next()
                C["o"].next(3)
                use.next(n)
                use_no[0] += n

            def mixing(l):
                norm(l, 0, 1, norm_mem["f"])
                for hh in range(2):
                    if hh == 0:
                        act.wait_ge(s_gath, 16 * P)
                    act.wait_ge(s_free, use.at(-1))
                    srcs = [(G[:, :, :, :], a["gath_lh"][l * 2 + hh]), (V[:, 8, :], a["cv"][l * 2 + hh])]
                    if hh == 0:
                        srcs += [(ckT[:, :, :], a["ck"][l]), (mask[:, :, :], a["mask"])]
                    for dst, src in srcs:
                        act.dma_start(dst, src).then_inc(s_att, 16)
                        C["att"].next(16)
                    skip(4)
                    for t in range(5):
                        act.wait_ge(s_full, C["full"].next())
                        if t < 3:
                            i = act.activation(V[0:64, 4 + t, :], bank(use_no[0], 0, 0, 256, 64, 128), ACT.Copy)
                        if 0 < t < 4:
                            i = act.activation(V[64:128, 3 + t, :], bank(use_no[0], 0, 0, 256, 0, 64), ACT.Copy)
                        if t < 4:
                            i.then_inc(s_func, 1)
                            C["func"].next()
                        use.next()
                        use_no[0] += 1
                    ada_pair()
                    ada_pair()
                    act.wait_ge(s_free, use.at())
                    act.dma_start(a["new_k"][l * 2 + hh], kT[:, :, LAT:T]).then_inc(s_kv, 16)
                    act.dma_start(a["new_v"][l * 2 + hh], V[:, 7, :]).then_inc(s_kv, 16)
                    C["kv"].next(32)
                    attention(hh)
                skip(10)
                skip(14)

                def gates(i):
                    for pair in range(2):
                        for m in range(2):
                            for h in range(2):
                                u = use_no[0]
                                act.wait_ge(s_full, C["full"].next())
                                act.wait_ge(s_free, use.at(3))
                                for b in range(2):
                                    q = act.activation(sig[:, m * 2 + h, b, :], bank(u, b, 0, HT), ACT.Sigmoid)
                                q.then_inc(s_func, 1)
                                C["func"].next()
                                use.next()
                                use_no[0] += 1
                        skip(4)
                        for _ in range(1 + pair):
                            ada_pair()

                start = use_no[0]
                over(act, 2, [(use, 16), (C["full"], 16), (C["func"], 8), (C["ada"], 6)], gates, act_met)
                use_no[0] = start + 32
                over(act, 2, [(C["ada"], 2)], lambda i: ada_pair(), act_met)
                last_products(l, 1, norm_mem["m"])

            def layer(l):
                use_no[0] = 0
                ffn(l, 0, False)
                mixing(l)
                ffn(l, 2, True)
                norm(l, 2, 1, norm_mem["f"])

            act.dma_start(craw[:, 0, :], a["c"].partition_broadcast(P)).then_inc(s_csilu, 16)
            act.dma_start(craw[:, 1, :], a["c_ctx"].partition_broadcast(P)).then_inc(s_csilu, 16)
            act.dma_start(bada[:, :], a["bada"]).then_inc(s_csilu, 16)
            load_ada(FIRST_ADA, 0)
            act.wait_ge(s_csilu, 48)
            act.activation(csilu[:, :, :], craw[:, :, :], ACT.Silu).then_inc(s_csilu, 16)
            act.wait_ge(s_mods, 1)
            act.wait_ge(s_x, 16 * KD)
            for h in range(2):
                for k in range(KD):
                    if h * KD + k >= 4:
                        act.wait_ge(s_u, h * KD + k - 3)
                    for lo, hi, v in SEGS[h]:
                        i = act.activation(norm_mem["f"][1][:, k % 4, lo - h * HT:hi - h * HT], X[:, k, lo:hi],
                                           ACT.Identity, bias=mods[0][:, v, k:k + 1],
                                           scale=mods[0][:, v, KD + k:KD + k + 1])
                    i.then_inc(s_u32, 1)
            over_layers(act, list(C.values()), layer)
            act.wait_ge(s_kv, DEPTH * PER_LAYER["kv"])
            act.wait_ge(s_aload[0], (DEPTH * 3 * ADA_SUB // 2 + 1) * 16)

        @block.vector
        def _(dve):
            C = make("use full func h mods u32 u mean sum sq sqsum added std xc xn att kv max cc exp p pt o mix mrg ada dve".split())
            use = C["use"]
            use_no = [0]

            def link(i):
                i.then_inc(s_dve, 1)
                dve.wait_ge(s_dve, C["dve"].next())

            def mark(i, name):
                i.then_inc(C[name].sem, 1)
                C[name].next()

            def free(i):
                i.then_inc(s_free, 1)
                use.next()
                use_no[0] += 1

            def ada_pair(target, where, loaded, at=None):
                for s in range(2):
                    dve.wait_ge(s_aload[s], loaded)
                    link(dve.tensor_tensor_reduce(junk[:, :], ada_w[:, s, :], csilu[:, 0, :], 1.0, 0.0, ALU.mult,
                                                  ALU.add, acc4[:, 0, s:s + 1]))
                    i = dve.tensor_tensor_reduce(junk[:, :], ada_w[:, s, :], csilu[:, 1, :], 1.0, 0.0,
                                                 ALU.mult, ALU.add, acc4[:, 1, s:s + 1])
                    i.then_inc(s_adone, 1)
                    C["ada"].next()
                    dve.wait_ge(s_adone, C["ada"].at())
                link(dve.tensor_copy(target[:, :, bass.ds(where, 2)], acc4[:, :, :]))

            def finish_gate(m, q, weight):
                for v in range(2):
                    i = dve.tensor_tensor(m[:, v, 2 * KD:], m[:, v, 2 * KD:], bada[:, bass.ds(q, KD)], ALU.add)
                link(i)
                if weight != 1.0:
                    link(dve.tensor_scalar(m[:, :, 2 * KD:], m[:, :, 2 * KD:], weight, None, ALU.mult))

            def finish_mods(m, q, ln=None):
                for v in range(2):
                    i = dve.tensor_tensor(m[:, v, 0:2 * KD], m[:, v, 0:2 * KD], bada[:, bass.ds(q, 2 * KD)], ALU.add)
                link(i)
                i = dve.tensor_scalar(m[:, :, KD:2 * KD], m[:, :, KD:2 * KD], 1.0, None, ALU.add)
                if ln is not None:
                    link(i)
                    for v in range(2):
                        g, b = [t[:, bass.ds(ln, KD)] for t in (lng0, lnb0)]
                        dve.tensor_tensor(lnm[:, v, 0, :], m[:, v, KD:2 * KD], g, ALU.mult)
                        link(dve.tensor_tensor(lnm[:, v, 1, :], m[:, v, KD:2 * KD], b, ALU.mult))
                        i = dve.tensor_tensor(lnm[:, v, 1, :], lnm[:, v, 1, :], m[:, v, 0:KD], ALU.add)
                mark(i, "mods")
                dve.wait_ge(s_mods, C["mods"].at())

            def split_u(h, k, u32):
                dve.wait_ge(s_u32, C["u32"].next())
                cols = slice(h * HT, (h + 1) * HT)
                link(dve.tensor_copy(Uh[:, k, cols], u32[:, k % 4, :]))
                mark(dve.tensor_tensor(Ul[:, k, cols], u32[:, k % 4, :], Uh[:, k, cols].bitcast(F32),
                                       ALU.subtract), "u")

            def add_pair(m, h, pair, mem):
                u, total = use_no[0], mem[3][:, h, :]
                dve.wait_ge(s_full, C["full"].next())
                for b in range(2):
                    n = 2 * pair + b
                    for lo, hi, v in SEGS[h]:
                        x = X[:, n, lo:hi]
                        i = dve.scalar_tensor_tensor(x, bank(u, b, lo - h * HT, hi - h * HT),
                                                     m[:, v, 2 * KD + n:2 * KD + n + 1], x, ALU.mult, ALU.add)
                free(i)
                dve.wait_ge(s_free, use.at())
                x0, x1 = [X[:, 2 * pair + b, h * HT:(h + 1) * HT] for b in range(2)]
                if pair == 0:
                    link(dve.tensor_tensor(total, x0, x1, ALU.add))
                else:
                    link(dve.tensor_tensor(total, total, x0, ALU.add))
                    i = dve.tensor_tensor(total, total, x1, ALU.add)
                    if pair < KD // 2 - 1:
                        link(i)
                    else:
                        mark(i, "sum")

            def centre(h, mem):
                u, sq, total = use_no[0], mem[2], mem[4][:, h, :]
                dve.wait_ge(s_mean, C["mean"].next())

                def centred(k):
                    x = X[:, k, h * HT:(h + 1) * HT]
                    mark(dve.tensor_tensor(x, x, bank(u, 0, 0, HT), ALU.subtract), "xc")

                def add(k):
                    if k == 1:
                        C["sq"].next()
                    dve.wait_ge(s_sq, C["sq"].next())
                    if k > 1:
                        dve.wait_ge(s_added, C["added"].at())
                    i = dve.tensor_tensor(total, sq[:, 0, :] if k == 1 else total, sq[:, k % 4, :], ALU.add)
                    if k == KD - 1:
                        mark(i, "sqsum")
                    else:
                        mark(i, "added")

                for k in range(KD):
                    centred(k)
                    if k >= 2:
                        add(k - 1)
                add(KD - 1)

            def normalise(h, mem, between=()):
                std, u32 = mem[:2]
                dve.wait_ge(s_std, C["std"].next())
                free(dve.reciprocal(std[:, h, :], std[:, h, :]))
                dve.wait_ge(s_free, use.at())

                def normed(k):
                    x = X[:, k, h * HT:(h + 1) * HT]
                    mark(dve.tensor_tensor(x, x, std[:, h, :], ALU.mult), "xn")

                ahead = 2
                for k in range(ahead):
                    normed(k)
                for k in range(KD):
                    if k + ahead < KD:
                        normed(k + ahead)
                    split_u(h, k, u32)
                    if k in (2, 5, 7) and between:
                        between[(2, 5, 7).index(k)]()

            def last_products(l, s, mem, next_q):
                nxt = (s + 1) % 3
                dve.wait_ge(s_free, use.at())
                for pair in range(KD // 2):
                    add_pair(mods[s], 0, pair, mem)
                centre(0, mem)
                finish_mods(mods[nxt], next_q, l * (3 * KD) + s * KD)
                normalise(0, mem, [lambda pair=pair: add_pair(mods[s], 1, pair, mem) for pair in range(3)])
                add_pair(mods[s], 1, 3, mem)

            def pending_norm(mem):
                centre(1, mem)
                normalise(1, mem)

            def down(m, n_of, count):
                for n in range(count):
                    u = use_no[0]
                    dve.wait_ge(s_full, C["full"].next())
                    dve.wait_ge(s_free, use.at())
                    for h in range(2):
                        for lo, hi, v in SEGS[h]:
                            x = X[:, bass.ds(n_of(n), 1), lo:hi].rearrange("p a n -> p (a n)")
                            g = m[:, v, bass.ds(n_of(n) + 2 * KD, 1)]
                            i = dve.scalar_tensor_tensor(x, bank(u, h, lo - h * HT, hi - h * HT), g, x,
                                                         ALU.mult, ALU.add)
                    free(i)

            def down_loop(m):
                start = use_no[0]
                over(dve, 2, [(use, 4), (C["full"], 4)], lambda i: down(m, lambda n: i * 4 + n, 4),
                     dve_met)
                use_no[0] = start + KD

            def ffn(l, s, pending):
                nxt = (s + 1) % 3
                if pending:
                    pending_norm(norm_mem["m"])
                base = C["ada"].n
                chunk = 0
                for group, size in enumerate(GROUPS):
                    target, col = ((mods[s], 2 * KD), (mods[nxt], 0), (mods[nxt], KD))[group]

                    def evacuate(at, h):
                        u = use_no[0]
                        b = u % 2
                        dve.wait_ge(s_func, C["func"].next())
                        C["full"].next()
                        free(dve.tensor_tensor(hf[:, b, :], sg[:, b, :], bank(u, 0, 0, HT), ALU.mult))
                        dve.wait_ge(s_free, use.at())
                        hh, hl = [t[:, at, h * HT:(h + 1) * HT] for t in (Hh, Hl)]
                        if not isinstance(at, int):
                            hh, hl = [t.rearrange("p a n -> p (a n)") for t in (hh, hl)]
                        link(dve.tensor_copy(hh, hf[:, b, :]))
                        mark(dve.tensor_tensor(hl, hf[:, b, :], hh.bitcast(F32), ALU.subtract), "h")

                    if group == 0:
                        for h in range(2):
                            for m in range(2):
                                evacuate(m, h)
                        ada_pair(target, col, loads(l, base, 0))
                    done = 2 * (group == 0)

                    def up(i):
                        for m in range(2):
                            for h in range(2):
                                evacuate(bass.ds(i * 2 + (m + done), 1), h)
                        ada_pair(target, i * 2 + (col + done), loads(l, base + chunk + done, i))

                    start = use_no[0]
                    n = (size - done) // 2
                    over(dve, n, [(use, 4), (C["full"], 4), (C["func"], 4), (C["h"], 4), (C["ada"], 2),
                                  (C["dve"], 4 + 3)], up, dve_met)
                    use_no[0] = start + 4 * n
                    chunk += size
                    if group == 0:
                        finish_gate(mods[s], l * (3 * ADA_SUB) + (s * ADA_SUB + 2 * KD), 0.5)
                    if group < 2:
                        down_loop(mods[s])
                ada_pair(mods[nxt], KD + size, loads(l, base + chunk, 0))
                last_products(l, s, norm_mem["f"], l * (3 * ADA_SUB) + (s + 1) * ADA_SUB)

            def loads(l, chunk, i):
                return (l * (3 * ADA_SUB) + (i * 2 + (chunk + 2))) * 8

            def attention(hh):
                units = [(h, j) for h in range(4) for j in range(QB)] + [(h, QB) for h in range(4)]
                u0, n = use_no[0], len(units)
                for i in range(n + 3):
                    if i < n:
                        h, j = units[i]
                        s3 = pr[:, i % 3, :]
                        if j == 0:
                            for kind in range(3):
                                g = G[:, h, :, BIAS_OFF[kind]:BIAS_OFF[kind] + WCOLS].rearrange("p r t -> p t r")
                                q = dve.tensor_tensor(bm[:, kind, :].rearrange("p (t r) -> p t r", r=ROWS), g,
                                                      mask[:, kind, :].rearrange("p (t r) -> p t r", r=ROWS), ALU.add)
                            link(q)
                        if i >= 3:
                            dve.wait_ge(s_pt, C["pt"].next())
                        dve.wait_ge(s_full, C["full"].next())
                        if j < QB:
                            link(dve.tensor_tensor(s3[:, 0:256], bank(u0 + i, 0, 0, 256), bm[:, BIAS_KIND[j], :],
                                                   ALU.add))
                            dve.wait_ge(s_cc, C["cc"].next())
                        else:
                            link(dve.tensor_copy(s3[:, 0:P], bank(u0 + i, 0, 0, P)))
                        w = 384 if j < QB else P
                        link(dve.tensor_reduce(stat[:, i % 4, 0:1], s3[:, 0:w], AX_X, ALU.max))
                        mark(dve.tensor_scalar(stat[:, i % 4, 1:2], stat[:, i % 4, 0:1], -1.0, None, ALU.mult), "max")
                    if 1 <= i <= n:
                        b = i - 1
                        w = 384 if units[b][1] < QB else P
                        dve.wait_ge(s_exp, C["exp"].next())
                        link(dve.reciprocal(stat[:, b % 4, 3:4], stat[:, b % 4, 2:3]))
                        mark(dve.tensor_scalar(pr[:, b % 3, 0:w], pr[:, b % 3, 0:w], stat[:, b % 4, 3:4], None,
                                               ALU.mult), "p")
                    if 3 <= i:
                        h, j = units[i - 3]
                        po, chunk = HD * (h % 2), 2 * hh + h // 2
                        dve.wait_ge(s_o, C["o"].next())
                        free(dve.tensor_copy(o32[po:po + HD, chunk, j * P:(j + 1) * P],
                                             bank(u0 + i - 3, 0, 384, 512, po, po + HD)))
                C["pt"].next(3)

            def split_from(src, hi, lo):
                link(dve.tensor_copy(hi, src))
                return dve.tensor_tensor(lo, src, hi.bitcast(F32), ALU.subtract)

            def mixing(l):
                pending_norm(norm_mem["f"])
                base = C["ada"].n
                chunk = 0
                for hh in range(2):
                    for m in range(4):
                        u = use_no[0]
                        dve.wait_ge(s_full, C["full"].next())
                        dst = qT if m < 2 else kT
                        for h in range(2):
                            i = dve.tensor_scalar(dst[:, m % 2, h * HT:(h + 1) * HT], bank(u, h, 0, HT),
                                                  ATTN_SCALE if m < 2 else 1.0, None, ALU.mult)
                        free(i)
                    for t in range(5):
                        u = use_no[0]
                        dve.wait_ge(s_full, C["full"].next())
                        if t < 4:
                            dve.wait_ge(s_func, C["func"].next())
                        i = dve.tensor_copy(V[:, t if t < 4 else 7, :], bank(u, 0, 0, 256))
                        free(i)
                    for _ in range(2):
                        ada_pair(mods[1], 2 * KD + chunk, loads(l, base + chunk, 0))
                        chunk += 2
                    dve.wait_ge(s_att, C["att"].next(64 if hh == 0 else 32))
                    attention(hh)
                    dve.wait_ge(s_kv, C["kv"].next(32))
                for part in range(2):
                    for t in range(5):
                        u = use_no[0]
                        dve.wait_ge(s_full, C["full"].next())
                        cols = slice(part * 256, part * 256 + 256)
                        free(split_from(bank(u, 0, 0, 256), Fh[:, t, cols], Fl[:, t, cols]))
                for part in range(2):
                    for g in range(4):
                        u = use_no[0]
                        dve.wait_ge(s_full, C["full"].next())
                        hi, lo = ((PCh, PCl), (PSh, PSl))[part]
                        free(split_from(bank(u, 0, 0, LAT), hi[:, g, :], lo[:, g, :]))
                for g in range(4):
                    u = use_no[0]
                    dve.wait_ge(s_full, C["full"].next())
                    free(dve.tensor_copy(y32[:, g, 0:LAT], bank(u, 0, 0, LAT)))
                u = use_no[0]
                dve.wait_ge(s_full, C["full"].next())
                for b in range(2):
                    i = split_from(bank(u, b, 0, 512).rearrange("p (g n) -> p g n", g=2),
                                   CXh[:, 2 * b:2 * b + 2, :], CXl[:, 2 * b:2 * b + 2, :])
                free(i)
                u = use_no[0]
                dve.wait_ge(s_full, C["full"].next())
                free(dve.tensor_copy(y32[:, :, LAT:T], bank(u, 0, 0, LAT).rearrange("p (g n) -> p g n", g=4)))
                dve.wait_ge(s_free, use.at())
                link(dve.tensor_copy(Oh[:, :, :], o32[:, :, :]))
                link(dve.tensor_tensor(Ol[:, :, :], o32[:, :, :], Oh[:, :, :].bitcast(F32), ALU.subtract))
                link(dve.tensor_copy(Yh[:, :, :], y32[:, :, :]))
                mark(dve.tensor_tensor(Yl[:, :, :], y32[:, :, :], Yh[:, :, :].bitcast(F32), ALU.subtract), "mix")
                dve.wait_ge(s_mix, C["mix"].at())

                def gates(i):
                    for pair in range(2):
                        for _ in range(4):
                            dve.wait_ge(s_func, C["func"].next())
                            C["full"].next()
                            dve.wait_ge(s_free, use.at())
                            dve.sem_inc(s_free, 1)
                            use.next()
                            use_no[0] += 1
                        for m in range(2):
                            for h in range(2):
                                u = use_no[0]
                                s = sig[:, m * 2 + h, :, :]
                                dve.wait_ge(s_full, C["full"].next())
                                dve.tensor_tensor(ta[:, 0, :], s[:, 0, :], bank(u, 0, 0, HT), ALU.mult)
                                free(dve.tensor_tensor(ta[:, 1, :], s[:, 1, :], bank(u, 1, 0, HT), ALU.mult))
                                dve.wait_ge(s_free, use.at())
                                dst = M32[:, bass.ds(i * 4 + (pair * 2 + m), 1), h * HT:(h + 1) * HT]
                                link(dve.tensor_tensor(dst.rearrange("p a n -> p (a n)"), ta[:, 0, :], ta[:, 1, :],
                                                       ALU.add))
                        if pair == 0:
                            ada_pair(mods[2], i * 6, loads(l, base + chunk, i * 3))
                        else:
                            for e in (2, 4):
                                ada_pair(mods[2], i * 6 + e, loads(l, base + chunk + e, i * 3))

                start = use_no[0]
                over(dve, 2, [(use, 16), (C["full"], 16), (C["func"], 8), (C["ada"], 6), (C["dve"], 8 + 9)], gates,
                     dve_met)
                use_no[0] = start + 32
                chunk += 12
                link(dve.tensor_copy(Mh[:, :, :], M32[:, :, :]))
                mark(dve.tensor_tensor(Ml[:, :, :], M32[:, :, :], Mh[:, :, :].bitcast(F32), ALU.subtract), "mrg")
                dve.wait_ge(s_mrg, C["mrg"].at())
                over(dve, 2, [(C["ada"], 2), (C["dve"], 3)],
                     lambda i: ada_pair(mods[2], i * 2 + 12, loads(l, base + chunk, i)), dve_met)
                finish_gate(mods[1], l * (3 * ADA_SUB) + (ADA_SUB + 2 * KD), 1.0)
                last_products(l, 1, norm_mem["m"], l * (3 * ADA_SUB) + 2 * ADA_SUB)

            def layer(l):
                use_no[0] = 0
                ffn(l, 0, False)
                mixing(l)
                ffn(l, 2, True)
                pending_norm(norm_mem["f"])

            for c in C.values():
                c.base, c.n = 0, 0
            dve.memset(epsc[:, :], LN_EPS)
            dve.memset(ones[:, :], 1.0 / D).then_inc(s_init, 1)
            dve.wait_ge(s_cst, 64)
            dve.tensor_copy(cst_h[:, :, :], cst[:, :, :]).then_inc(s_init, 1)
            dve.wait_ge(s_init, 2)
            dve.tensor_tensor(cst_l[:, :, :], cst[:, :, :], cst_h[:, :, :].bitcast(F32), ALU.subtract)\
                .then_inc(s_init, 1)
            dve.wait_ge(s_init, 3)
            dve.drain().then_inc(s_free, 4)
            dve.wait_ge(s_csilu, 64)
            for c in range(FIRST_ADA):
                dve.wait_ge(s_ada0[c // 4], 16)
                if c:
                    dve.wait_ge(s_dve, C["dve"].at())
                dve.tensor_tensor_reduce(junk[:, :], ada0[:, c, :], csilu[:, 0, :], 1.0, 0.0, ALU.mult,
                                         ALU.add, mods[0][:, 0, c:c + 1]).then_inc(s_dve, 1)
                C["dve"].next()
                dve.wait_ge(s_dve, C["dve"].at())
                dve.tensor_tensor_reduce(ada0[:, c, :], ada0[:, c, :], csilu[:, 1, :], 1.0, 0.0, ALU.mult,
                                         ALU.add, mods[0][:, 1, c:c + 1])
            link(dve.drain())
            dve.sem_inc(s_adone, 1)
            finish_mods(mods[0], 0)
            for h in range(2):
                for k in range(KD):
                    split_u(h, k, norm_mem["f"][1])
            dve.tensor_copy(lng0[:, :], lng[:, :])
            dve.tensor_copy(lnb0[:, :], lnb[:, :])
            link(dve.tensor_scalar(X[:, :, :], X[:, :, :], ALPHA, None, ALU.mult))
            n = (DEPTH * 3 - 1) * KD
            dve.tensor_scalar(lng[:, 0:n], lng[:, 0:n], ALPHA, None, ALU.mult)
            link(dve.tensor_scalar(lnb[:, 0:n], lnb[:, 0:n], ALPHA, None, ALU.mult))
            assert C["dve"].n == FIRST_DVE, C["dve"].n
            over_layers(dve, list(C.values()), layer)


NORMS = 3 * 2 * KD
UNITS = HEADS * (QB + 1)
PER_LAYER = dict(
    tile=TILES, use=USES, full=USES - 6, func=112, h=88, mods=3, u32=NORMS, u=NORMS, mean=6, sum=6, sqsum=6,
    added=6 * (KD - 2), var=6, std=6, xc=NORMS, sq=NORMS,
    xn=NORMS, y=NORMS, att=96, max=UNITS, cc=UNITS - HEADS, exp=UNITS, p=UNITS, pt=UNITS, ptc=UNITS, o=UNITS,
    mix=1, mrg=1, kv=64, ada=3 * ADA_SUB, dve=465)
FIRST_DVE = 36


def block(w, k, m):
    return w[k * P:(k + 1) * P, m * P:(m + 1) * P]


def weight_stream(w):
    deg = 2 * np.pi / LAT
    tok = (np.arange(LAT) % ROWS) * GRID_W + np.arange(LAT) // ROWS
    ang = deg * ((tok[:, None] * tok[None, :]) % LAT)
    waves = [(f(ang) / np.sqrt(LAT * P)).astype(np.float32).reshape(4, P, LAT).transpose(1, 0, 2).reshape(P, 16, P)
             for f in (np.cos, np.sin)]
    tiles = []

    def blocks(bs):
        for i in range(0, len(bs), 16):
            tiles.append(np.stack(bs[i:i + 16], axis=1))

    def ffn(up, dn):
        first = 0
        for size in GROUPS:
            for m in range(first, first + size):
                blocks([block(up, k, c) for c in (m, FF // P + m) for k in range(KD)])
            for _ in range(1 if first + size < FF // P else 2):
                blocks([block(dn, k, n) for n in range(KD) for k in range(first, first + size)])
            first += size

    def columns(wi, lo):
        tiles.append(wi[:, lo:lo + 256].reshape(KD, P, 256).transpose(1, 0, 2).reshape(P, 16, P))

    for l in range(DEPTH):
        ffn(w["w_ff1_up"][l], w["w_ff1_down"][l])
        wi = w["w_in"][l]
        for hh in range(2):
            for c in (0, NA // P):
                blocks([block(wi, k, c + 2 * hh + m) for m in range(2) for k in range(KD)])
            columns(wi, 2 * NA + 256 * hh)
        for part in range(2):
            columns(wi, 3 * NA + 256 * part)
        tiles.extend(waves)
        c0 = 4 * NA // P
        for m in range(0, KD, 2):
            for n in (m, m + 1):
                blocks([block(wi, k, c) for c in (c0 + n, c0 + KD + n) for k in range(KD)])
            blocks([block(v[l], k, n) for n in (m, m + 1) for v in (w["w_fourier"], w["w_na_out"]) for k in range(4)])
        for _ in range(2):
            blocks([block(w["w_out"][l], k, n) for n in range(KD) for k in range(KD)])
        ffn(w["w_ff2_up"][l], w["w_ff2_down"][l])
    assert len(tiles) == DEPTH * TILES
    return np.stack(tiles)


def window_masks():
    out = np.zeros((P, 3, WCOLS, ROWS), np.float32)
    for kind, j in ((0, 0), (1, 1), (2, 3)):
        for c in range(QTILE):
            first = min(max(QTILE * j + c - WIN // 2, 0), GRID_W - WIN)
            for t in range(WCOLS):
                if not first <= KEY0[j] + t < first + WIN:
                    out[c * ROWS:(c + 1) * ROWS, kind, t, :] = NEG
    return out.reshape(P, 3, WCOLS * ROWS)


def small_waves():
    ang = 2 * np.pi / P * (np.outer(np.arange(P), np.arange(P)) % P)
    return np.stack([np.cos(ang), -np.sin(ang), np.cos(ang) / P, np.sin(ang) / P], axis=1).astype(np.float32)


OUTS = {"yT": (KD, P, T), "new_k": (2 * DEPTH, P, 2, P), "new_v": (2 * DEPTH, P, 256)}


def arrays_of(x):
    lat = x["x_sample"][0].reshape(ROWS, GRID_W, D).transpose(1, 0, 2).reshape(LAT, D)
    tokens = np.concatenate([lat, x["x_prompt"][0]], axis=0)
    ck = x["cache_k"][0].reshape(DEPTH, 4, 2, P, HD).transpose(0, 2, 4, 1, 3).reshape(DEPTH, P, 4, P)
    cv = x["cache_v"][0].reshape(DEPTH, 2, 4, P, HD).transpose(0, 1, 3, 2, 4).reshape(2 * DEPTH, P, 256)
    ada = x["w_ada"].transpose(0, 2, 1).reshape(DEPTH * 3 * ADA_SUB, P, D)
    bada = x["b_ada"].reshape(DEPTH * 3 * ADA_SUB, P)
    return {
        "xT": np.ascontiguousarray(tokens.T).reshape(KD, P, T),
        "c": x["c"][0], "c_ctx": x["c_ctx"],
        "wstream": weight_stream(x),
        "ada": np.concatenate([ada, np.zeros((FIRST_ADA + 1, P, D), np.float32)]),
        "bada": np.ascontiguousarray(np.concatenate([bada, np.zeros((ADA_SUB, P), np.float32)]).T),
        "lng": np.ascontiguousarray(x["ln_g"].reshape(DEPTH * 3 * KD, P).T),
        "lnb": np.ascontiguousarray(x["ln_b"].reshape(DEPTH * 3 * KD, P).T),
        "rpb": np.pad(x["rpb"].reshape(DEPTH * HEADS, 2 * ROWS - 1, 2 * WIN - 1), ((0, 0), (0, 0), (16, 17))),
        "ck": np.ascontiguousarray(ck), "cv": np.ascontiguousarray(cv),
        "dft_small": small_waves(), "eye": np.eye(P, dtype=np.float32), "mask": window_masks(),
    }


def program(nc, arrays):
    a = {n: nc.dram_tensor("in_" + n, v.shape, F32, kind="ExternalInput").ap() for n, v in arrays.items()}
    for n, shape in OUTS.items():
        a[n] = nc.dram_tensor(n, shape, F32, kind="ExternalOutput").ap()
    a["gath"] = nc.dram_tensor("gath", (DEPTH * HEADS, P, ROWS, TW), F32, kind="Internal").ap()
    a["gath_lh"] = a["gath"].rearrange("(q h) p r t -> q p h r t", h=4)
    build(nc, a)


def outputs_of(r):
    y = np.asarray(r["yT"]).reshape(D, T).T
    y_s = y[:LAT].reshape(GRID_W, ROWS, D).transpose(1, 0, 2).reshape(1, LAT, D)
    y_p = y[LAT:].reshape(1, CTX, D)
    nk = np.asarray(r["new_k"]).reshape(DEPTH, 2, 2, HD, 2, P).transpose(0, 1, 4, 2, 5, 3)
    nv = np.asarray(r["new_v"]).reshape(DEPTH, 2, P, 4, HD).transpose(0, 1, 3, 2, 4)
    shape = (1, DEPTH, HEADS, P, HD)
    return tuple(np.ascontiguousarray(v) for v in (y_p, y_s, nk.reshape(shape), nv.reshape(shape)))


def kernel(**inputs):
    import concourse.bacc as _bacc
    from concourse.bass_utils import run_bass_kernel_spmd as _run

    arrays = arrays_of({n: np.asarray(v) for n, v in inputs.items()})
    arrays = {n: np.ascontiguousarray(v) for n, v in arrays.items()}
    nc = _bacc.Bacc("TRN2", target_bir_lowering=False, num_devices=1)
    program(nc, arrays)
    r = _run(nc, [{"in_" + n: v for n, v in arrays.items()}], core_ids=[0])
    return outputs_of(r.results[0])
```
